# Optimizing a Trainium2 kernel written in Bass

```python
import jax, jax.numpy as jnp
from jax import lax
import numpy as np

D_MODEL = 1024
BATCH = 1
SEQ = 256
DEPTH = 2

CHUNK = 64
POOL_WIDTH = D_MODEL // 4
POOL_WINDOWS = (2, 4, 8, 16)
POOL_GROUPS = len(POOL_WINDOWS)
POOL_GROUP_DIM = POOL_WIDTH // POOL_GROUPS
CONV_WIDTH = D_MODEL // 4
CONV_KERNEL = 31
ATTN_HEADS = 8
HEAD_DIM = 64
ATTN_WIDTH = ATTN_HEADS * HEAD_DIM
N_BRANCH = 3
Q_BLOCK = 128
D_FF = 2816
N_EXPERTS = 8
TOP_K = 2
D_FF_EXPERT = 3584
EPS = 1e-6
N_DENSE = (DEPTH + 1) // 2
N_MOE = DEPTH // 2

OFF_POOL = 0
OFF_CONV = OFF_POOL + POOL_WIDTH
OFF_Q = OFF_CONV + 2 * CONV_WIDTH
OFF_K = OFF_Q + ATTN_WIDTH
OFF_V = OFF_K + ATTN_WIDTH
OFF_F = OFF_V + ATTN_WIDTH
OFF_G = OFF_F + ATTN_HEADS
IN_COLS = OFF_G + N_BRANCH * D_MODEL

kernel_name = "hybrid_pool_conv_fox_moe_trunk"

def rms_norm(x, g):
    xf = x.astype(jnp.float32)
    y = xf * lax.rsqrt(jnp.mean(xf * xf, axis=-1, keepdims=True) + EPS)
    return (y * g.astype(jnp.float32)).astype(x.dtype)

def layer_norm(x, g, b):
    xf = x.astype(jnp.float32)
    mu = jnp.mean(xf, axis=-1, keepdims=True)
    var = jnp.mean(jnp.square(xf - mu), axis=-1, keepdims=True)
    y = (xf - mu) * lax.rsqrt(var + EPS)
    return (y * g.astype(jnp.float32) + b.astype(jnp.float32)).astype(x.dtype)

def pool_mixer(p, w_group, scale):
    S = p.shape[1]
    pf = p.astype(jnp.float32)
    cs = jnp.cumsum(pf, axis=1)
    t = jnp.arange(1, S + 1, dtype=jnp.float32)
    outs = []
    for g, w in enumerate(POOL_WINDOWS):
        lo, hi = g * POOL_GROUP_DIM, (g + 1) * POOL_GROUP_DIM
        csg = cs[..., lo:hi]
        lagged = jnp.pad(csg, ((0, 0), (w, 0), (0, 0)))[:, :S]
        count = jnp.minimum(t, float(w))[None, :, None]
        pooled = (csg - lagged) / count - pf[..., lo:hi]
        outs.append(jnp.einsum('bsc,cd->bsd', pooled.astype(p.dtype), w_group[g]))
    return jnp.concatenate(outs, axis=-1) * scale

def conv_module(u, conv_w, conv_b, ln_g, ln_b):
    a, gate = jnp.split(u, 2, axis=-1)
    z = a * jax.nn.sigmoid(gate)
    z = lax.conv_general_dilated(
        z, conv_w[:, None, :].astype(z.dtype), window_strides=(1,),
        padding=[(CONV_KERNEL - 1, 0)], dimension_numbers=('NWC', 'WIO', 'NWC'),
        feature_group_count=CONV_WIDTH) + conv_b
    z = layer_norm(z, ln_g, ln_b)
    return jax.nn.silu(z)

def forgetting_attention(q, k, v, f_logit, q_g, k_g):
    B, S, H, Dh = q.shape
    q = rms_norm(q, q_g)
    k = rms_norm(k, k_g)
    logf = jax.nn.log_sigmoid(f_logit.astype(jnp.float32))
    c = jnp.transpose(jnp.cumsum(logf, axis=1), (0, 2, 1))
    nb = S // Q_BLOCK
    qb = q.reshape(B, nb, Q_BLOCK, H, Dh).transpose(1, 0, 3, 2, 4)
    cqb = c.reshape(B, H, nb, Q_BLOCK).transpose(2, 0, 1, 3)
    kpos = jnp.arange(S)
    scale = HEAD_DIM ** -0.5

    def block(args):
        qi, cqi, i = args
        s = jnp.einsum('bhqd,bshd->bhqs', qi, k, preferred_element_type=jnp.float32) * scale
        s = s + (cqi[..., None] - c[:, :, None, :])
        qpos = i * Q_BLOCK + jnp.arange(Q_BLOCK)
        s = jnp.where(kpos[None, :] <= qpos[:, None], s, -jnp.inf)
        prob = jax.nn.softmax(s, axis=-1).astype(v.dtype)
        return jnp.einsum('bhqs,bshd->bhqd', prob, v)

    o = lax.map(block, (qb, cqb, jnp.arange(nb)))
    return o.transpose(1, 0, 3, 2, 4).reshape(B, S, H * Dh)

def swiglu(h, w1, w3, w2):
    a = jnp.einsum('bsd,df->bsf', h, w1)
    b = jnp.einsum('bsd,df->bsf', h, w3)
    return jnp.einsum('bsf,fd->bsd', jax.nn.silu(a) * b, w2)

def moe_ffn(h, w_router, w1, w3, w2):
    logits = jnp.einsum('bsd,de->bse', h, w_router, preferred_element_type=jnp.float32)
    top_val, top_idx = lax.top_k(logits, TOP_K)
    top_w = jax.nn.softmax(top_val, axis=-1)
    gates = jnp.sum(jax.nn.one_hot(top_idx, N_EXPERTS, dtype=jnp.float32) * top_w[..., None], axis=-2)
    gates = gates.astype(h.dtype)
    out = jnp.zeros_like(h)
    for e in range(N_EXPERTS):
        out = out + gates[..., e:e + 1] * swiglu(h, w1[e], w3[e], w2[e])
    return out

def setup_inputs(seed: int = 0) -> dict:
    key = jax.random.key(seed)
    ks = jax.random.split(key, 32)
    L, D = DEPTH, D_MODEL
    nrm = lambda k, shape, fan_in: jax.random.normal(k, shape, jnp.float32) * (fan_in ** -0.5)
    gain = lambda k, shape: 1.0 + 0.05 * jax.random.normal(k, shape, jnp.float32)
    small = lambda k, shape: 0.02 * jax.random.normal(k, shape, jnp.float32)
    return {
        "x": jax.random.normal(ks[0], (BATCH, SEQ, D), jnp.float32),
        "g_mix": gain(ks[1], (L, D)),
        "w_in": nrm(ks[2], (L, D, IN_COLS), D),
        "b_gate": small(ks[3], (L, N_BRANCH * D)),
        "b_forget": jax.random.uniform(ks[4], (L, ATTN_HEADS), jnp.float32, 1.0, 6.0),
        "pool_w": nrm(ks[5], (L, POOL_GROUPS, POOL_GROUP_DIM, POOL_GROUP_DIM), POOL_GROUP_DIM),
        "pool_scale": gain(ks[6], (L, POOL_WIDTH)),
        "conv_w": nrm(ks[7], (L, CONV_KERNEL, CONV_WIDTH), CONV_KERNEL),
        "conv_b": small(ks[8], (L, CONV_WIDTH)),
        "conv_ln_g": gain(ks[9], (L, CONV_WIDTH)),
        "conv_ln_b": small(ks[10], (L, CONV_WIDTH)),
        "q_norm_g": gain(ks[11], (L, HEAD_DIM)),
        "k_norm_g": gain(ks[12], (L, HEAD_DIM)),
        "w_br_pool": nrm(ks[13], (L, POOL_WIDTH, D), POOL_WIDTH),
        "w_br_conv": nrm(ks[14], (L, CONV_WIDTH, D), CONV_WIDTH),
        "w_br_attn": nrm(ks[15], (L, ATTN_WIDTH, D), ATTN_WIDTH),
        "w_out": nrm(ks[16], (L, D, D), D),
        "g_ffn": gain(ks[17], (L, D)),
        "ffn_w1": nrm(ks[18], (N_DENSE, D, D_FF), D),
        "ffn_w3": nrm(ks[19], (N_DENSE, D, D_FF), D),
        "ffn_w2": nrm(ks[20], (N_DENSE, D_FF, D), D_FF),
        "router_w": nrm(ks[21], (N_MOE, D, N_EXPERTS), D),
        "exp_w1": nrm(ks[22], (N_MOE, N_EXPERTS, D, D_FF_EXPERT), D),
        "exp_w3": nrm(ks[23], (N_MOE, N_EXPERTS, D, D_FF_EXPERT), D),
        "exp_w2": nrm(ks[24], (N_MOE, N_EXPERTS, D_FF_EXPERT, D), D_FF_EXPERT),
    }

def reference(x, g_mix, w_in, b_gate, b_forget, pool_w, pool_scale, conv_w, conv_b,
              conv_ln_g, conv_ln_b, q_norm_g, k_norm_g, w_br_pool, w_br_conv, w_br_attn,
              w_out, g_ffn, ffn_w1, ffn_w3, ffn_w2, router_w, exp_w1, exp_w3, exp_w2):
    B, S, D = x.shape
    for l in range(DEPTH):
        h = rms_norm(x, g_mix[l])
        u = jnp.einsum('bsd,dc->bsc', h, w_in[l])
        y_pool = pool_mixer(u[..., OFF_POOL:OFF_CONV], pool_w[l], pool_scale[l])
        y_conv = conv_module(u[..., OFF_CONV:OFF_Q], conv_w[l], conv_b[l], conv_ln_g[l], conv_ln_b[l])
        q = u[..., OFF_Q:OFF_K].reshape(B, S, ATTN_HEADS, HEAD_DIM)
        k = u[..., OFF_K:OFF_V].reshape(B, S, ATTN_HEADS, HEAD_DIM)
        v = u[..., OFF_V:OFF_F].reshape(B, S, ATTN_HEADS, HEAD_DIM)
        f_logit = u[..., OFF_F:OFF_G] + b_forget[l]
        y_attn = forgetting_attention(q, k, v, f_logit, q_norm_g[l], k_norm_g[l])
        gates = jax.nn.sigmoid(u[..., OFF_G:] + b_gate[l]).reshape(B, S, N_BRANCH, D)
        merged = (gates[:, :, 0] * jnp.einsum('bsc,cd->bsd', y_pool, w_br_pool[l])
                  + gates[:, :, 1] * jnp.einsum('bsc,cd->bsd', y_conv, w_br_conv[l])
                  + gates[:, :, 2] * jnp.einsum('bsc,cd->bsd', y_attn, w_br_attn[l]))
        x = x + jnp.einsum('bsd,de->bse', merged, w_out[l])
        h = rms_norm(x, g_ffn[l])
        if l % 2 == 0:
            i = l // 2
            x = x + swiglu(h, ffn_w1[i], ffn_w3[i], ffn_w2[i])
        else:
            i = l // 2
            x = x + moe_ffn(h, router_w[i], exp_w1[i], exp_w3[i], exp_w2[i])
    return x


_drawn_inputs = setup_inputs


def setup_inputs(seed=0):
    import zlib

    import numpy as np

    out = dict(_drawn_inputs(seed))
    spreads = {}
    factors = {'b_gate': 2.678, 'conv_ln_b': 2.748, 'k_norm_g': 3.007}
    for name, (base, spread) in spreads.items():
        noise = np.random.default_rng([zlib.crc32(name.encode()), seed]).standard_normal(out[name].shape)
        drawn = base * np.exp(spread * noise) if base else spread * noise
        out[name] = __import__('jax').numpy.asarray(drawn.astype(out[name].dtype))
    for name, factor in factors.items():
        out[name] = (out[name] * factor).astype(out[name].dtype)
    return out
```

```python
from contextlib import ExitStack

import numpy as np

import concourse.bass as bass
from concourse import mybir

F32 = mybir.dt.float32
F32R = mybir.dt.float32r
I32 = mybir.dt.int32
U32 = mybir.dt.uint32
ALU = mybir.AluOpType
ACT = mybir.ActivationFunctionType
AX_X = mybir.AxisListType.X

P = 128
D = 1024
KC = D // P
S = 256
TT = S // P
DEPTH = 2
HEADS = 8
HD = 64
WINDOWS = (2, 4, 8, 16)
TAPS = 31
PAD = TAPS - 1
CONVC = 2
OFF_POOL, OFF_CONV, OFF_Q, OFF_K, OFF_V, OFF_F, OFF_G = 0, 256, 768, 1280, 1792, 2304, 2312
D_FF = 2816
D_EXP = 3584
EXPERTS = 8
EXTRA_JOBS = 3
EPS = 1e-6
NEG = -1e30

RAW = 6
SPLIT = 3
PIECE = 2048

C_IDENT, C_HALVES, C_UPTO, C_ONES, C_AFTER, C_BEFORE, C_MASK, C_IOTA, C_POOL = range(9)
N_CONST = C_POOL + 3 * len(WINDOWS)

A_GMIX, A_GFFN, A_BGATE, A_PSCALE, A_CONVW, A_CONVB, A_LNG, A_LNB, A_QG, A_KG, A_BF = (
    0, 8, 16, 40, 42, 104, 106, 108, 110, 111, 112)
A_EPS, A_EPS64, A_POOLW, A_WF, A_ROUTER = 120, 121, 122, 378, 442
N_PARAM = 506

P_CONV, P_Q, P_K, P_V, P_POOL, P_GATE, P_BRPOOL, P_BRCONV, P_BRATTN, P_OUT = 0, 2, 4, 6, 8, 9, 21, 22, 23, 25
MIX_PIECES = 29
DENSE_BLOCKS = D_FF // S
DENSE_PIECES = 3 * DENSE_BLOCKS
EXP_BLOCKS = D_EXP // 512
JOB_PIECES = 6 * EXP_BLOCKS
BASE = [0, MIX_PIECES + DENSE_PIECES]
DENSE0 = MIX_PIECES
MOE0 = BASE[1] + MIX_PIECES

UNITS = 37
ACT_UNITS = [1, 6, 7, 8] + list(range(9, 21))
DVE_UNITS = [0, 2, 3, 4, 5] + list(range(21, 37))
UNIT_PIECE = list(range(21)) + [21] * 4 + [22] * 4 + [23] * 2 + [24] * 2 + list(range(25, 29))
UNIT_LAST = [u + 1 == UNITS or UNIT_PIECE[u + 1] != UNIT_PIECE[u] for u in range(UNITS)]
PARTS = UNIT_LAST.count(False)
HIGH_ORDER = {0: 1, 4: 2, 5: 3, 6: 4, 7: 5, 2: 6}
LOW_ORDER = {0: 1, 4: 2, 5: 3, 6: 4, 2: 5, 7: 6}


def pieces_of_mixer(l, w_in, w_br_pool, w_br_conv, w_br_attn, w_out):
    win = w_in[l].rearrange("(k p) n -> p k n", p=P)
    wout = w_out[l].rearrange("(k p) n -> p k n", p=P)
    attn = w_br_attn[l].rearrange("(k p) n -> p k n", p=P)
    columns = [OFF_CONV, OFF_CONV + 256, OFF_Q, OFF_Q + 256, OFF_K, OFF_K + 256, OFF_V, OFF_V + 256, OFF_POOL]
    columns += [OFF_G + 256 * i for i in range(12)]
    out = [(win[:, :, c:c + 256], KC) for c in columns]
    out += [(w_br_pool[l].rearrange("(k p) n -> p k n", p=P), 2), (w_br_conv[l].rearrange("(k p) n -> p k n", p=P), 2)]
    out += [(attn[:, :, 512 * i:512 * i + 512], 4) for i in range(2)]
    out += [(wout[:, :, 256 * i:256 * i + 256], KC) for i in range(4)]
    assert len(out) == MIX_PIECES
    return out


def trunk(nc, xt, consts, params, w_in, w_br_pool, w_br_conv, w_br_attn, w_out,
          ffn_w1, ffn_w3, ffn_w2, exp_w1, exp_w3, exp_w2, out):
    with ExitStack() as ctx:
        def sb(name, shape, dt=F32):
            return ctx.enter_context(nc.sbuf_tensor(name, shape, dt))

        def sem(name):
            return ctx.enter_context(nc.semaphore(name))

        bank = [ctx.enter_context(nc.psum_tensor(f"bank{i}", [P, 512], F32)) for i in range(8)]

        raw = [sb(f"raw{i}", [P, PIECE]) for i in range(RAW)]
        wh = [sb(f"w_high{i}", [P, PIECE], F32R) for i in range(SPLIT)]
        wl = [sb(f"w_low{i}", [P, PIECE], F32R) for i in range(SPLIT)]
        xT = sb("xT", [P, KC, S])
        hf = sb("h_full", [P, KC, S])
        hH = sb("h_high", [P, KC, S], F32R)
        hL = sb("h_low", [P, KC, S], F32R)
        cst = sb("cst", [P, N_CONST, P])
        par = sb("par", [P, DEPTH, N_PARAM])
        rt = sb("rt", [P, 512])
        rinv = sb("rinv", [P, 512])
        wfH = sb("wf_high", [P, 128], F32R)
        wfL = sb("wf_low", [P, 128], F32R)

        with ExitStack() as mix:
            def mb(name, shape, dt=F32):
                return mix.enter_context(nc.sbuf_tensor(name, shape, dt))

            fg = mb("fg", [P, 6, TT * HEADS])
            half = mb("half_bias", [P, 24])
            gate = mb("gate", [P, 24, S])
            zp = mb("zp", [P, CONVC, PAD + S])
            cv = mb("cv", [P, CONVC, S])
            cs = mb("cs", [P, CONVC, S])
            vt = mb("vt", [P, TT, 512])
            decay = mb("decay", [P, 2, 3, P])
            negmax = mb("negmax", [P, 2, 2])
            psum_ = mb("prob_sum", [P, 2, 2])
            pinv = mb("prob_inv", [P, 2, 2])
            prob = mb("prob", [P, 2, 384])
            probT = mb("probT", [P, 384])
            yH = mb("y_high", [P, 8, S], F32R)
            yL = mb("y_low", [P, 8, S], F32R)
        yf = cs
        qk = hf
        qsq = gate[:, 20:24, :].rearrange("p a b -> p (a b)").rearrange("p (u n) -> p u n", u=2)
        pt_ = gate[:, 18:20, :]
        pooled = gate[:, 16:18, :]

        zero = sb("zero", [P, 512], F32R)
        sl = sb("sl", [P, 512])
        gu = sb("gu", [P, 512])
        gH = sb("g_high", [P, 512], F32R)
        gL = sb("g_low", [P, 512], F32R)
        htH = sb("ht_high", [P, TT, D], F32R)
        htL = sb("ht_low", [P, TT, D], F32R)
        hgH = sb("hg_high", [P, KC, P], F32R)
        hgL = sb("hg_low", [P, KC, P], F32R)
        xacc = sb("xacc", [P, TT, D])
        ysb = sb("ysb", [P, D])
        permG = sb("perm_gated", [P, TT, P])
        permT = sb("perm_t", [P, S])
        perm = sb("perm", [P, TT, P], F32R)
        lg = sb("lg", [P, TT, 8])
        top = sb("top", [P, TT, 8])
        topi = sb("topi", [P, TT, 8], U32)
        topf = sb("topf", [P, TT, 8])
        wt = sb("wt", [P, 4, TT])
        pick = sb("pick", [P, 2, TT, 8])
        tmp8 = sb("tmp8", [P, TT, 8])
        cnt = sb("cnt", [P, 6, 8])
        over = sb("over", [P, EXTRA_JOBS, 8])
        jobs = sb("jobs", [P, 3, TT, 12])
        jobf = sb("jobf", [P, 16])
        jobi = sb("jobi", [P, 16], I32)

        names = """const_in x_in high_done split_done used
            squares norm_stats norm_root norm_h h_high_done h_low_done norm_step
            f_logits f_soft decay_in decays unit_part ln_taps unit_used_act unit_used_dve conv_sig z_ready
            qk_sq qk_stats qk_root qk_ready v_ready pool_stats pool_in_ready pooled_ready pool_lin
            y_full y_high_done y_low_done ln_mean ln_zc ln_sq ln_var ln_root ln_v ln_th
            scores max_done exp_done prob_done prob_t prob_t_out pv merged merged_high merged_low
            dve_step act_step wf_high wf_low zeros
            d_silu d_mult d_high d_low d_res
            r_logits r_lg r_exp r_pick r_rank r_tables fill fill_act fill_dve
            m_zero m_silu m_mult m_t m_high m_low m_yout m_gather m_gout m_perm m_permt m_ptout
            m_comb m_add jobs_ready stored""".split()
        s = {n: sem(n) for n in names}
        raw_in = [sem(f"raw_in{i}") for i in range(RAW)]

        def C(i, n=1):
            return cst[:, i:i + n, :].rearrange("p a b -> p (a b)")

        def A(l, i, n=1):
            return par[:, l, i:i + n]

        ident = C(C_IDENT)

        def fold(ap, k):
            return ap.rearrange("p (k n) -> p k n", k=k)

        def num(c, r):
            return c if isinstance(r, int) and r == 0 else r * RAW + c

        def unit_ready(eng, l, u):
            if UNIT_LAST[u]:
                eng.wait_ge(s["used"], BASE[l] + UNIT_PIECE[u] + 1)
            else:
                eng.wait_ge(s["unit_part"], PARTS * l + UNIT_LAST[:u + 1].count(False))

        def x_ready(eng, nn):
            if nn == 0:
                eng.wait_ge(s["x_in"], 16)
            elif nn == 2:
                eng.wait_ge(s["d_res"], 4)
            else:
                eng.wait_ge(s["unit_used_dve"], len(DVE_UNITS) * (nn // 2 + 1))

        def load_piece(sp, c, r, src, k):
            if not (isinstance(r, int) and c < RAW):
                sp.wait_ge(s["split_done"], num(c - RAW + 1, r))
            sp.dma_start(fold(raw[c % RAW][:], k), src).then_inc(raw_in[c % RAW], 16)

        def split_high(act, c, r=0):
            act.wait_ge(raw_in[c % RAW], 16 * (c // RAW + 1) if isinstance(r, int) else r * 16 + 16 * (c // RAW + 1))
            if not (isinstance(r, int) and c < SPLIT):
                act.wait_ge(s["used"], num(c - SPLIT + 1, r))
            nc.scalar.activation(wh[c % SPLIT][:], raw[c % RAW][:], ACT.Copy).then_inc(s["high_done"], 1)

        def split_low(dve, c, r=0):
            dve.wait_ge(s["high_done"], num(c + 1, r))
            nc.vector.tensor_tensor(wl[c % SPLIT][:], raw[c % RAW][:], wh[c % SPLIT][:].bitcast(F32),
                                    ALU.subtract).then_inc(s["split_done"], 1)

        def take_piece(pe, c, r=0, k=KC):
            pe.wait_ge(s["split_done"], num(c + 1, r))
            return fold(wh[c % SPLIT][:], k), fold(wl[c % SPLIT][:], k)

        def products(pe, dst, terms, start=True, stop=True):
            for i, (lh, ll, rh, rl) in enumerate(terms):
                pe.matmul(dst, lh, rh, start=start and i == 0, stop=False)
                pe.matmul(dst, lh, rl, start=False, stop=False)
                last = pe.matmul(dst, ll, rh, start=False, stop=stop and i == len(terms) - 1)
            return last

        block = ctx.enter_context(nc.Block())

        @block.sync
        def _(sp):
            sp.dma_start(xT[:], xt).then_inc(s["x_in"], 16)
            sp.dma_start(par[:], params).then_inc(s["const_in"], 16)
            sp.dma_start(cst[:], consts).then_inc(s["const_in"], 16)
            d1 = ffn_w1[0].rearrange("(k p) n -> p k n", p=P)
            d3 = ffn_w3[0].rearrange("(k p) n -> p k n", p=P)
            d2 = ffn_w2[0].rearrange("(b k p) n -> b p k n", p=P, k=2)
            for l in range(DEPTH):
                for n, (src, k) in enumerate(pieces_of_mixer(l, w_in, w_br_pool, w_br_conv, w_br_attn, w_out)):
                    load_piece(sp, BASE[l] + n, 0, src, k)
                if l == 0:
                    load_piece(sp, DENSE0, 0, d1[:, :, 0:S], KC)
                    load_piece(sp, DENSE0 + 1, 0, d3[:, :, 0:S], KC)
                    with sp.Fori(0, (DENSE_BLOCKS - 1) // 2) as i:
                        for u in range(2):
                            c = DENSE0 + 2 + 3 * u
                            at = bass.ds(i * (2 * S) + (u + 1) * S, S)
                            load_piece(sp, c, i, d1[:, :, at], KC)
                            load_piece(sp, c + 1, i, d3[:, :, at], KC)
                            load_piece(sp, c + 2, i, d2[bass.ds(i * 2 + u, 1)].rearrange("b p k n -> (b p) k n"), 2)
                    load_piece(sp, DENSE0 + DENSE_PIECES - 1, 0, d2[DENSE_BLOCKS - 1], 2)
            e1 = exp_w1[0].rearrange("e (k p) n -> e p k n", p=P)
            e3 = exp_w3[0].rearrange("e (k p) n -> e p k n", p=P)
            e2 = exp_w2[0].rearrange("e (b k p) n -> e b p k n", p=P, k=2)
            sp.wait_ge(s["jobs_ready"], 1)
            njobs = sp.value_load(jobi[0:1, 12:13], min_val=EXPERTS, max_val=EXPERTS + EXTRA_JOBS)
            with sp.Fori(0, njobs) as j:
                e = sp.value_load(jobi[0:1, bass.ds(j, 1)], min_val=0, max_val=EXPERTS - 1)
                one = bass.ds(e, 1)

                def up(c, r, fb):
                    for w, k0 in ((e1, 0), (e1, 4), (e3, 0), (e3, 4)):
                        load_piece(sp, c, r, w[one, :, k0:k0 + 4, fb].rearrange("e p k n -> (e p) k n"), 4)
                        c += 1

                def down(c, r, b):
                    for u in range(2):
                        at = bass.ds(b + u, 1) if isinstance(b, int) else bass.ds(b + u, 1)
                        load_piece(sp, c + u, r, e2[one, at].rearrange("e b p k n -> (e b p) k n"), 2)

                up(MOE0, j * EXP_BLOCKS, bass.ds(0, 512))
                with sp.Fori(0, EXP_BLOCKS - 1) as i:
                    r = j * EXP_BLOCKS + i
                    up(MOE0 + 4, r, bass.ds(i * 512 + 512, 512))
                    down(MOE0 + 8, r, i * 2)
                down(MOE0 + JOB_PIECES - 2, j * EXP_BLOCKS, 2 * (EXP_BLOCKS - 1))
            sp.wait_ge(s["m_add"], njobs * 4 + 4)
            sp.dma_start(out.rearrange("b (t p) d -> p (b t) d", p=P), xacc[:]).then_inc(s["stored"], 16)
            sp.wait_ge(s["stored"], 16)

        @block.gpsimd
        def _(pool):
            for l in range(DEPTH):
                lf = fg[:, 5, :].rearrange("p (t h) -> p t h", t=TT)
                pool.wait_ge(s["decay_in"], l + 1)
                for h in range(HEADS):
                    if h >= 2:
                        pool.wait_ge(s["scores"], 8 * l + h - 1)
                    for k, (m, tile) in enumerate(((C_UPTO, 0), (C_UPTO, 1), (C_ONES, 0))):
                        nc.gpsimd.tensor_scalar(decay[:, h % 2, k, :], C(m), lf[:, tile, h:h + 1], None,
                                                ALU.mult).then_inc(s["decays"], 1)

        @block.scalar
        def _(act):
            def norm(nn, ahead):
                x_ready(act, nn)
                for g in range(2):
                    nc.scalar.activation(hf[:, 4 * g:4 * g + 4, :], xT[:, 4 * g:4 * g + 4, :],
                                         ACT.Square).then_inc(s["squares"], 1)
                for c in ahead[:2]:
                    split_high(act, c)
                act.wait_ge(s["norm_stats"], nn + 1)
                nc.scalar.activation(rt[:, 0:S], bank[3][:, 0:S], ACT.Sqrt, bias=A(0, A_EPS),
                                     scale=1.0 / D).then_inc(s["norm_root"], 1)
                for g in range(4):
                    act.wait_ge(s["norm_h"], 8 * nn + 2 * g + 2)
                    nc.scalar.activation(hH[:, 2 * g:2 * g + 2, :], hf[:, 2 * g:2 * g + 2, :],
                                         ACT.Copy).then_inc(s["h_high_done"], 1)
                for c in ahead[2:]:
                    split_high(act, c)

            def mixer(l):
                b = BASE[l]
                norm(2 * l, [b, b + 1, b + 2])
                act.wait_ge(s["f_soft"], 2 * l + 1)
                nc.scalar.activation(fg[:, 2, :], fg[:, 1, :], ACT.Exp, scale=-1.0).then_inc(s["act_step"], 1)
                act.wait_ge(s["act_step"], 2 * l + 1)
                nc.scalar.activation(fg[:, 3, :], fg[:, 2, :], ACT.Ln, bias=C(C_ONES)[:, 0:1]).then_inc(s["act_step"], 1)

                def gate_out(u):
                    unit_ready(act, l, u)
                    for m in range(2):
                        g = 2 * (u - P_GATE) + m
                        ins = nc.scalar.activation(gate[:, g, :], bank[u % 3][:, m * S:m * S + S], ACT.Tanh,
                                                   bias=half[:, g:g + 1], scale=0.5)
                    ins.then_inc(s["unit_used_act"], 1)

                for n in range(3, MIX_PIECES):
                    if n == 4:
                        unit_ready(act, l, 1)
                        nc.scalar.activation(cs[:].rearrange("p c t -> p (c t)"), bank[1][:], ACT.Tanh,
                                             scale=0.5).then_inc(s["unit_used_act"], 1)
                    if 6 <= n <= 9:
                        u = n - 4
                        act.wait_ge(s["qk_stats"], 4 * l + u - 1)
                        if u > P_Q:
                            act.wait_ge(s["unit_used_dve"], len(DVE_UNITS) * l + DVE_UNITS.index(u - 1) + 1)
                        q = u < P_K
                        nc.scalar.activation(rt[:], bank[6 + u % 2][:], ACT.Sqrt,
                                             bias=A(0, A_EPS64 if q else A_EPS),
                                             scale=1.0 if q else 1.0 / HD).then_inc(s["qk_root"], 1)
                    if 5 <= n <= 8:
                        u = n - 3
                        unit_ready(act, l, u)
                        nc.scalar.activation(qsq[:, u % 2, :], bank[u % 3][:], ACT.Square).then_inc(s["qk_sq"], 1)
                    if 9 <= n <= 11:
                        u = n - 3
                        unit_ready(act, l, u)
                        dst = pt_[:] if u == P_POOL else vt[:, :, 256 * (u - P_V):256 * (u - P_V) + 256]
                        nc.scalar.activation(dst, fold(bank[u % 3][:], 2), ACT.Copy).then_inc(s["unit_used_act"], 1)
                    if n == 13:
                        act.wait_ge(s["pooled_ready"], l + 1)
                        nc.scalar.activation(pooled[:], fold(bank[3][:], 2), ACT.Copy).then_inc(s["pool_in_ready"], 1)
                    if n == 15:
                        act.wait_ge(s["y_full"], 2 * l + 1)
                        nc.scalar.activation(yH[:, 0:2, :], yf[:], ACT.Copy).then_inc(s["y_high_done"], 1)
                    if 12 <= n <= 23:
                        gate_out(n - 3)
                    if 14 <= n <= 21:
                        h = n - 14
                        act.wait_ge(s["max_done"], 2 * (8 * l + h) + 2)
                        for t, (a, z) in enumerate(((0, 128), (128, 384))):
                            nc.scalar.activation(prob[:, h % 2, a:z], bank[4 + h % 2][:, a:z], ACT.Exp,
                                                 bias=negmax[:, h % 2, t:t + 1],
                                                 accum_out=psum_[:, h % 2, t:t + 1]).then_inc(s["exp_done"], 1)
                    if 16 <= n <= 23:
                        h = n - 16
                        act.wait_ge(s["prob_t"], 8 * l + h + 1)
                        if h:
                            act.wait_ge(s["pv"], 8 * l + h)
                        nc.scalar.activation(probT[:], bank[6][:, 0:384], ACT.Copy).then_inc(s["prob_t_out"], 1)
                    if n >= 18 and n <= 24 and n % 2 == 0:
                        c = (n - 18) // 2
                        act.wait_ge(s["pv"], 8 * l + 2 * c + 2)
                        nc.scalar.activation(yH[:, 4 + c, :], bank[7][:, 0:S], ACT.Copy).then_inc(s["y_high_done"], 1)
                    if n == 20:
                        act.wait_ge(s["ln_zc"], 2 * l + 2)
                        nc.scalar.activation(cs[:], cv[:], ACT.Square).then_inc(s["ln_sq"], 1)
                    if n == 22:
                        act.wait_ge(s["ln_var"], l + 1)
                        nc.scalar.activation(rt[:, 0:S], bank[3][:, S:2 * S], ACT.Sqrt, bias=A(0, A_EPS),
                                             scale=1.0 / 256).then_inc(s["ln_root"], 1)
                    if n == 23:
                        act.wait_ge(s["ln_v"], 2 * l + 2)
                        nc.scalar.activation(cs[:], cv[:], ACT.Tanh, scale=0.5).then_inc(s["ln_th"], 1)
                    if n == 24:
                        act.wait_ge(s["y_full"], 2 * l + 2)
                        nc.scalar.activation(yH[:, 2:4, :], yf[:], ACT.Copy).then_inc(s["y_high_done"], 1)
                    if n == 27:
                        for m in range(4):
                            act.wait_ge(s["merged"], 4 * l + m + 1)
                            nc.scalar.activation(hH[:, 2 * m:2 * m + 2, :], hf[:, 2 * m:2 * m + 2, :], ACT.Copy,
                                                 scale=0.5).then_inc(s["merged_high"], 1)
                    split_high(act, b + n)

            def dense():
                norm(1, [DENSE0, DENSE0 + 1])

                def block_steps(par_, before):
                    act.wait_ge(s["used"], before * 3 + (DENSE0 + 2))
                    nc.scalar.activation(sl[:], bank[par_][:], ACT.Silu).then_inc(s["d_silu"], 1)
                    act.wait_ge(s["d_mult"], before + 1)
                    nc.scalar.activation(gH[:], gu[:], ACT.Copy).then_inc(s["d_high"], 1)

                with act.Fori(0, (DENSE_BLOCKS - 1) // 2) as i:
                    for u in range(2):
                        c = DENSE0 + 2 + 3 * u
                        split_high(act, c, i)
                        split_high(act, c + 1, i)
                        block_steps(u, i * 2 + u)
                        split_high(act, c + 2, i)
                split_high(act, DENSE0 + DENSE_PIECES - 1)
                block_steps(0, DENSE_BLOCKS - 1)

            def experts():
                norm(3, [])
                for f in range(8):
                    act.wait_ge(s["fill"], f + 1)
                    dst = (htH if f < 4 else htL)[:, f % 4 // 2, 512 * (f % 2):512 * (f % 2) + 512]
                    nc.scalar.activation(dst, bank[f % 7][:], ACT.Copy).then_inc(s["fill_act"], 1)
                act.wait_ge(s["r_lg"], 1)
                nc.scalar.activation(wt[:, 1, :], wt[:, 0, :], ACT.Exp).then_inc(s["r_exp"], 1)

                def gather_out(g, count):
                    act.wait_ge(s["m_gather"], count + g + 1)
                    dst = (hgH if g < 2 else hgL)[:, 4 * (g % 2):4 * (g % 2) + 4, :]
                    nc.scalar.activation(dst, fold(bank[(5, 6, 7, 5)[g]][:], 4), ACT.Copy).then_inc(s["m_gout"], 1)

                def y_out(j):
                    act.wait_ge(s["m_zero"], 1)
                    act.wait_ge(s["used"], j * JOB_PIECES + MOE0)
                    for h in range(2):
                        nc.scalar.activation(ysb[:, 512 * h:512 * h + 512], bank[2 + h][:], ACT.Copy).then_inc(s["m_yout"], 1)

                def t_high(count):
                    act.wait_ge(s["m_t"], count)
                    nc.scalar.activation(gH[:], bank[4][:], ACT.Copy).then_inc(s["m_high"], 1)

                def silu(up_done):
                    act.wait_ge(s["used"], up_done)
                    nc.scalar.activation(sl[:], bank[0][:], ACT.Silu).then_inc(s["m_silu"], 1)

                for g in range(4):
                    gather_out(g, 0)
                act.wait_ge(s["jobs_ready"], 1)
                njobs = act.value_load(jobi[0:1, 12:13], min_val=EXPERTS, max_val=EXPERTS + EXTRA_JOBS)
                with act.Fori(0, njobs) as j:
                    r0, c = j * EXP_BLOCKS, MOE0
                    split_high(act, c, r0)
                    split_high(act, c + 1, r0)
                    split_high(act, c + 2, r0)
                    y_out(j)
                    split_high(act, c + 3, r0)
                    silu(j * JOB_PIECES + (MOE0 + 2))
                    split_high(act, c + 4, r0)
                    split_high(act, c + 5, r0)
                    with act.Fori(0, EXP_BLOCKS - 1) as i:
                        r = j * EXP_BLOCKS + i
                        split_high(act, c + 6, r)
                        split_high(act, c + 7, r)
                        split_high(act, c + 8, r)
                        t_high(r + 1)
                        silu(r * RAW + (MOE0 + 6))
                        split_high(act, c + 9, r)
                        split_high(act, c + 10, r)
                        split_high(act, c + 11, r)
                    for g in range(3):
                        gather_out(g, j * 4 + 4)
                    t_high(j * EXP_BLOCKS + EXP_BLOCKS)
                    gather_out(3, j * 4 + 4)
                    act.wait_ge(s["m_permt"], j + 1)
                    nc.scalar.activation(permT[:], bank[6][:, 0:S], ACT.Copy).then_inc(s["m_ptout"], 1)
                y_out(njobs)

            act.wait_ge(s["const_in"], 32)
            for l in range(DEPTH):
                nc.scalar.activation(half[:], A(l, A_BGATE, 24), ACT.Copy, scale=0.5).then_inc(s["wf_high"], 1)
                nc.scalar.activation(wfH[:], A(l, A_WF, 128), ACT.Copy).then_inc(s["wf_high"], 1)
                mixer(l)
                dense() if l == 0 else experts()

        @block.vector
        def _(dve):
            steps = [0]

            def step(ins):
                ins.then_inc(s["dve_step"], 1)
                steps[0] += 1

            def stepped():
                dve.wait_ge(s["dve_step"], steps[0])

            def norm(nn, ahead):
                for c in ahead[:1]:
                    split_low(dve, c)
                dve.wait_ge(s["norm_root"], nn + 1)
                nc.vector.reciprocal(rinv[:, 0:S], rt[:, 0:S]).then_inc(s["norm_step"], 1)
                dve.wait_ge(s["norm_step"], nn + 1)
                for k in range(KC):
                    nc.vector.scalar_tensor_tensor(
                        out=hf[:, k, :], in0=xT[:, k, :], scalar=A(nn // 2, (A_GMIX, A_GFFN)[nn % 2] + k),
                        in1=rinv[:, 0:S], op0=ALU.mult, op1=ALU.mult).then_inc(s["norm_h"], 1)
                for g in range(4):
                    dve.wait_ge(s["h_high_done"], 4 * nn + g + 1)
                    nc.vector.tensor_tensor(hL[:, 2 * g:2 * g + 2, :], hf[:, 2 * g:2 * g + 2, :],
                                            hH[:, 2 * g:2 * g + 2, :].bitcast(F32),
                                            ALU.subtract).then_inc(s["h_low_done"], 1)
                for c in ahead[1:]:
                    split_low(dve, c)

            def mixer(l):
                b = BASE[l]
                norm(2 * l, [b, b + 1, b + 2])
                step(nc.vector.memset(zp[:, :, 0:PAD], 0.0))
                dve.wait_ge(s["f_logits"], l + 1)
                step(nc.vector.tensor_tensor(
                    fg[:, 0, :].rearrange("p (t h) -> p t h", t=TT), bank[3][:, 256:272].rearrange("p (t h) -> p t h", t=TT),
                    A(l, A_BF, 8).unsqueeze(1).to_broadcast([P, TT, HEADS]), ALU.add))
                stepped()
                nc.vector.scalar_tensor_tensor(out=fg[:, 1, :], in0=fg[:, 0, :], scalar=-1.0, in1=fg[:, 0, :],
                                               op0=ALU.mult, op1=ALU.max).then_inc(s["f_soft"], 1)
                nc.vector.tensor_scalar(fg[:, 4, :], fg[:, 0, :], 0.0, None, ALU.min).then_inc(s["f_soft"], 1)

                taps = [(c, k) for k in range(TAPS) for c in range(CONVC)]
                tapped = [0]

                def run_taps(n):
                    for c, k in taps[tapped[0]:tapped[0] + n]:
                        tapped[0] += 1
                        w = A(l, A_CONVW + c * TAPS + k)
                        if k == 0:
                            step(nc.vector.tensor_scalar(cv[:, c, :], zp[:, c, 0:S], w, A(l, A_CONVB + c), ALU.mult, ALU.add))
                            continue
                        dve.wait_ge(s["dve_step"], steps[0] - (k < TAPS - 1))
                        ins = nc.vector.scalar_tensor_tensor(out=cv[:, c, :], in0=zp[:, c, k:k + S], scalar=w,
                                                             in1=cv[:, c, :], op0=ALU.mult, op1=ALU.add)
                        if k < TAPS - 1:
                            step(ins)
                        else:
                            ins.then_inc(s["ln_taps"], 1)

                def head_max(h):
                    dve.wait_ge(s["scores"], 8 * l + h + 1)
                    for t, (a, z) in enumerate(((0, 128), (128, 384))):
                        nc.vector.tensor_reduce(negmax[:, h % 2, t:t + 1], bank[4 + h % 2][:, a:z], AX_X, ALU.max,
                                                negate=True).then_inc(s["max_done"], 1)

                def head_norm(h):
                    dve.wait_ge(s["exp_done"], 2 * (8 * l + h) + 2)
                    step(nc.vector.reciprocal(pinv[:, h % 2, :], psum_[:, h % 2, :]))
                    stepped()
                    for t, (a, z) in enumerate(((0, 128), (128, 384))):
                        nc.vector.tensor_scalar(prob[:, h % 2, a:z], prob[:, h % 2, a:z], pinv[:, h % 2, t:t + 1],
                                                None, ALU.mult).then_inc(s["prob_done"], 1)

                def branch(u):
                    br, m = divmod(u - 21, 4)
                    unit_ready(dve, l, u)
                    dst = hf[:, 2 * m:2 * m + 2, :]
                    g = gate[:, 8 * br + 2 * m:8 * br + 2 * m + 2, :]
                    to = dst if br == 0 else g
                    ins = nc.vector.scalar_tensor_tensor(out=to, in0=g, scalar=1.0, in1=fold(bank[u % 3][:], 2),
                                                         op0=ALU.add, op1=ALU.mult)
                    ins.then_inc(s["unit_used_dve"], 1)
                    if br:
                        dve.wait_ge(s["unit_used_dve"], len(DVE_UNITS) * l + DVE_UNITS.index(u) + 1)
                        ins = nc.vector.tensor_tensor(dst, dst, g, ALU.add)
                        if br == 2:
                            ins.then_inc(s["merged"], 1)
                        else:
                            step(ins)

                def residual(u):
                    m = u - 33
                    unit_ready(dve, l, u)
                    nc.vector.tensor_tensor(xT[:, 2 * m:2 * m + 2, :], xT[:, 2 * m:2 * m + 2, :],
                                            fold(bank[u % 3][:], 2), ALU.add).then_inc(s["unit_used_dve"], 1)

                for n in range(3, MIX_PIECES):
                    if n == 4:
                        dve.wait_ge(s["unit_used_act"], len(ACT_UNITS) * l + 1)
                        step(nc.vector.tensor_scalar(cs[:], cs[:], 0.5, 0.5, ALU.mult, ALU.add))
                        stepped()
                        nc.vector.tensor_tensor(zp[:, :, PAD:], cs[:], fold(bank[0][:], 2),
                                                ALU.mult).then_inc(s["unit_used_dve"], 1)
                        dve.wait_ge(s["unit_used_dve"], len(DVE_UNITS) * l + 1)
                    if 6 <= n <= 9:
                        u = n - 4
                        dve.wait_ge(s["qk_root"], 4 * l + u - 1)
                        step(nc.vector.reciprocal(rinv[:], rt[:]))
                        stepped()
                        nc.vector.scalar_tensor_tensor(
                            out=qk[:, 2 * (u - 2):2 * (u - 2) + 2, :], in0=fold(bank[u % 3][:], 2),
                            scalar=A(l, A_QG if u < P_K else A_KG), in1=fold(rinv[:], 2),
                            op0=ALU.mult, op1=ALU.mult).then_inc(s["unit_used_dve"], 1)
                    if n == 7:
                        dve.wait_ge(s["act_step"], 2 * l + 2)
                        nc.vector.tensor_tensor(fg[:, 5, :], fg[:, 4, :], fg[:, 3, :],
                                                ALU.subtract).then_inc(s["decay_in"], 1)
                    if n == 14:
                        dve.wait_ge(s["pool_lin"], l + 1)
                        for c in range(2):
                            ins = nc.vector.tensor_scalar(yf[:, c, :], bank[3][:, c * S:c * S + S], A(l, A_PSCALE + c),
                                                          None, ALU.mult)
                        ins.then_inc(s["y_full"], 1)
                    if n == 16:
                        dve.wait_ge(s["y_high_done"], 6 * l + 1)
                        nc.vector.tensor_tensor(yL[:, 0:2, :], yf[:], yH[:, 0:2, :].bitcast(F32),
                                                ALU.subtract).then_inc(s["y_low_done"], 1)
                    if 14 <= n <= 21:
                        head_max(n - 14)
                    if 15 <= n <= 22:
                        head_norm(n - 15)
                    if n >= 19 and n <= 25 and n % 2 == 1:
                        c = (n - 19) // 2
                        dve.wait_ge(s["y_high_done"], 6 * l + HIGH_ORDER[4 + c])
                        nc.vector.tensor_tensor(yL[:, 4 + c, :], bank[7][:, 0:S], yH[:, 4 + c, :].bitcast(F32),
                                                ALU.subtract).then_inc(s["y_low_done"], 1)
                    if n == 19:
                        dve.wait_ge(s["ln_mean"], l + 1)
                        for c in range(CONVC):
                            nc.vector.scalar_tensor_tensor(out=cv[:, c, :], in0=bank[3][:, 0:S], scalar=-1.0 / 256,
                                                           in1=cv[:, c, :], op0=ALU.mult, op1=ALU.add).then_inc(s["ln_zc"], 1)
                    if n == 22:
                        dve.wait_ge(s["ln_root"], l + 1)
                        step(nc.vector.reciprocal(rinv[:, 0:S], rt[:, 0:S]))
                        stepped()
                        for c in range(CONVC):
                            step(nc.vector.scalar_tensor_tensor(out=cv[:, c, :], in0=cv[:, c, :], scalar=A(l, A_LNG + c),
                                                                in1=rinv[:, 0:S], op0=ALU.mult, op1=ALU.mult))
                        stepped()
                        for c in range(CONVC):
                            nc.vector.tensor_scalar(cv[:, c, :], cv[:, c, :], A(l, A_LNB + c), None,
                                                    ALU.add).then_inc(s["ln_v"], 1)
                    if n == 23:
                        dve.wait_ge(s["ln_th"], l + 1)
                        step(nc.vector.scalar_tensor_tensor(out=cs[:], in0=cs[:], scalar=1.0, in1=cv[:],
                                                            op0=ALU.add, op1=ALU.mult))
                        stepped()
                        nc.vector.tensor_scalar(yf[:], cs[:], 0.5, None, ALU.mult).then_inc(s["y_full"], 1)
                    if n == 24:
                        dve.wait_ge(s["y_high_done"], 6 * l + HIGH_ORDER[2])
                        nc.vector.tensor_tensor(yL[:, 2:4, :], yf[:], yH[:, 2:4, :].bitcast(F32),
                                                ALU.subtract).then_inc(s["y_low_done"], 1)
                        for u in range(21, 25):
                            branch(u)
                        stepped()
                    if n == 25:
                        for u in range(25, 29):
                            branch(u)
                        stepped()
                    if n == 26:
                        branch(29)
                        branch(30)
                    if n == 27:
                        branch(31)
                        branch(32)
                        for m in range(4):
                            dve.wait_ge(s["merged_high"], 4 * l + m + 1)
                            nc.vector.scalar_tensor_tensor(
                                out=hL[:, 2 * m:2 * m + 2, :], in0=hf[:, 2 * m:2 * m + 2, :], scalar=0.5,
                                in1=hH[:, 2 * m:2 * m + 2, :].bitcast(F32), op0=ALU.mult,
                                op1=ALU.subtract).then_inc(s["merged_low"], 1)
                    split_low(dve, b + n)
                    if 4 <= n <= 14:
                        run_taps(6)
                for u in range(33, 37):
                    residual(u)
                dve.wait_ge(s["unit_used_dve"], len(DVE_UNITS) * (l + 1))

            def dense():
                norm(1, [DENSE0, DENSE0 + 1])
                nc.vector.memset(zero[:].bitcast(F32), 0.0).then_inc(s["zeros"], 1)

                def block_steps(par_, before):
                    dve.wait_ge(s["d_silu"], before + 1)
                    nc.vector.tensor_tensor(gu[:], sl[:], bank[2 + par_][:], ALU.mult).then_inc(s["d_mult"], 1)
                    dve.wait_ge(s["d_high"], before + 1)
                    nc.vector.tensor_tensor(gL[:], gu[:], gH[:].bitcast(F32), ALU.subtract).then_inc(s["d_low"], 1)

                with dve.Fori(0, (DENSE_BLOCKS - 1) // 2) as i:
                    for u in range(2):
                        c = DENSE0 + 2 + 3 * u
                        split_low(dve, c, i)
                        split_low(dve, c + 1, i)
                        block_steps(u, i * 2 + u)
                        split_low(dve, c + 2, i)
                split_low(dve, DENSE0 + DENSE_PIECES - 1)
                block_steps(0, DENSE_BLOCKS - 1)
                dve.wait_ge(s["used"], BASE[1])
                for m in range(4):
                    nc.vector.tensor_tensor(xT[:, 2 * m:2 * m + 2, :], xT[:, 2 * m:2 * m + 2, :], fold(bank[4 + m][:], 2),
                                            ALU.add).then_inc(s["d_res"], 1)
                dve.wait_ge(s["d_res"], 4)

            def route():
                iota8 = C(C_IOTA)[:, 0:8]
                step(nc.vector.memset(jobs[:], 0.0))
                step(nc.vector.memset(jobf[:], 0.0))
                dve.wait_ge(s["r_logits"], 1)
                step(nc.vector.tensor_copy(lg[:], bank[7][:, 0:16].rearrange("p (t e) -> p t e", t=TT)))
                stepped()
                for t in range(TT):
                    step(nc.vector.max(top[:, t, :], lg[:, t, :]))
                stepped()
                for t in range(TT):
                    step(nc.vector.max_index(topi[:, t, :], top[:, t, :], lg[:, t, :]))
                nc.vector.tensor_tensor(wt[:, 0, :], top[:, :, 1], top[:, :, 0], ALU.subtract).then_inc(s["r_lg"], 1)
                stepped()
                step(nc.vector.tensor_copy(topf[:], topi[:]))
                stepped()
                for t in range(TT):
                    for a in range(2):
                        step(nc.vector.tensor_scalar(pick[:, a, t, :], iota8, topf[:, t, a:a + 1], None, ALU.is_equal))
                stepped()
                sel = jobs[:, 0, :, 0:8]
                nc.vector.tensor_tensor(sel, pick[:, 0], pick[:, 1], ALU.add).then_inc(s["r_pick"], 1)
                dve.wait_ge(s["r_exp"], 1)
                step(nc.vector.tensor_scalar(wt[:, 2, :], wt[:, 1, :], 1.0, None, ALU.add))
                stepped()
                step(nc.vector.reciprocal(wt[:, 3, :], wt[:, 2, :]))
                stepped()
                step(nc.vector.tensor_tensor(wt[:, 2, :], wt[:, 1, :], wt[:, 3, :], ALU.mult))
                stepped()
                for t in range(TT):
                    step(nc.vector.tensor_scalar(tmp8[:, t, :], pick[:, 1, t, :], wt[:, 2, t:t + 1], None, ALU.mult))
                stepped()
                for t in range(TT):
                    step(nc.vector.scalar_tensor_tensor(out=jobs[:, 2, t, 0:8], in0=pick[:, 0, t, :], scalar=wt[:, 3, t:t + 1],
                                                        in1=tmp8[:, t, :], op0=ALU.mult, op1=ALU.add))
                dve.wait_ge(s["r_rank"], 1)
                step(nc.vector.tensor_copy(jobs[:, 1, :, 0:8], bank[7][:, 32:48].rearrange("p (t e) -> p t e", t=TT)))
                step(nc.vector.tensor_copy(cnt[:, 0, :], bank[7][:, 64:72]))
                stepped()
                step(nc.vector.tensor_scalar(cnt[:, 1, :], cnt[:, 0, :], P + 0.5, None, ALU.is_gt))
                step(nc.vector.tensor_scalar(cnt[:, 4, :], iota8, -1.0, 16.0, ALU.mult, ALU.add))
                stepped()
                step(nc.vector.tensor_tensor(cnt[:, 2, :], cnt[:, 1, :], cnt[:, 4, :], ALU.mult))
                stepped()
                step(nc.vector.max(cnt[:, 3, :], cnt[:, 2, :]))
                step(nc.vector.tensor_reduce(cnt[:, 5, 0:1], cnt[:, 1, :], AX_X, ALU.add))
                stepped()
                for k in range(EXTRA_JOBS):
                    step(nc.vector.scalar_tensor_tensor(out=over[:, k, :], in0=cnt[:, 2, :], scalar=cnt[:, 3, k:k + 1],
                                                        in1=cnt[:, 1, :], op0=ALU.is_equal, op1=ALU.mult))
                stepped()
                for k in range(EXTRA_JOBS):
                    for q in range(3):
                        step(nc.vector.tensor_tensor(tmp8[:], jobs[:, q, :, 0:8],
                                                     over[:, k, :].unsqueeze(1).to_broadcast([P, TT, 8]), ALU.mult))
                        stepped()
                        step(nc.vector.tensor_reduce(jobs[:, q, :, 8 + k:9 + k], tmp8[:], AX_X, ALU.add))
                        stepped()
                step(nc.vector.tensor_scalar(jobs[:, 1, :, 8:8 + EXTRA_JOBS], jobs[:, 1, :, 8:8 + EXTRA_JOBS], -float(P), None, ALU.add))
                step(nc.vector.tensor_copy(jobf[:, 0:8], iota8))
                step(nc.vector.tensor_scalar(jobf[:, 8:8 + EXTRA_JOBS], cnt[:, 3, 0:EXTRA_JOBS], -1.0, 16.0, ALU.mult, ALU.add))
                step(nc.vector.tensor_scalar(jobf[:, 12:13], cnt[:, 5, 0:1], float(EXPERTS), None, ALU.add))
                stepped()
                step(nc.vector.tensor_scalar(jobf[:, 8:8 + EXTRA_JOBS], jobf[:, 8:8 + EXTRA_JOBS], float(EXPERTS - 1), None, ALU.min))
                stepped()
                nc.vector.tensor_copy(jobi[:], jobf[:]).then_inc(s["jobs_ready"], 1)

            def make_perm(q, dst, j, name):
                for t in range(TT):
                    nc.vector.tensor_scalar(dst[:, t, :], C(C_IOTA), jobs[:, 1, t, bass.ds(j, 1)], jobs[:, q, t, bass.ds(j, 1)],
                                            ALU.is_equal, ALU.mult).then_inc(s[name], 1)

            def add_rows(count):
                for q, b in enumerate((4, 7, 5, 6)):
                    dve.wait_ge(s["m_comb"], count + q + 1)
                    dst = xacc[:, q // 2, 512 * (q % 2):512 * (q % 2) + 512]
                    nc.vector.tensor_tensor(dst, dst, bank[b][:], ALU.add).then_inc(s["m_add"], 1)

            def experts():
                norm(3, [])
                nc.vector.memset(zero[:].bitcast(F32), 0.0).then_inc(s["zeros"], 1)
                nc.vector.memset(permT[:], 0.0).then_inc(s["m_ptout"], 1)
                route()
                stepped()
                make_perm(0, perm, 0, "m_perm")
                for f in range(8, 12):
                    dve.wait_ge(s["fill"], f + 1)
                    g = f - 8
                    nc.vector.tensor_copy(xacc[:, g // 2, 512 * (g % 2):512 * (g % 2) + 512],
                                          bank[f % 7][:]).then_inc(s["fill_dve"], 1)
                dve.wait_ge(s["fill_dve"], 4)
                dve.wait_ge(s["jobs_ready"], 1)
                njobs = dve.value_load(jobi[0:1, 12:13], min_val=EXPERTS, max_val=EXPERTS + EXTRA_JOBS)

                def mult(count, up_done):
                    dve.wait_ge(s["used"], up_done)
                    dve.wait_ge(s["m_silu"], count)
                    nc.vector.tensor_tensor(gu[:], sl[:], bank[1][:], ALU.mult).then_inc(s["m_mult"], 1)

                def t_low(count):
                    dve.wait_ge(s["m_high"], count)
                    nc.vector.tensor_tensor(gL[:], bank[4][:], gH[:].bitcast(F32), ALU.subtract).then_inc(s["m_low"], 1)

                with dve.Fori(0, njobs) as j:
                    r0, c = j * EXP_BLOCKS, MOE0
                    for k in range(4):
                        split_low(dve, c + k, r0)
                    mult(r0 + 1, j * JOB_PIECES + (MOE0 + 4))
                    split_low(dve, c + 4, r0)
                    split_low(dve, c + 5, r0)
                    add_rows(j * 4)
                    make_perm(0, perm, j + 1, "m_perm")
                    make_perm(2, permG, j, "m_perm")
                    with dve.Fori(0, EXP_BLOCKS - 1) as i:
                        r = j * EXP_BLOCKS + i
                        split_low(dve, c + 6, r)
                        split_low(dve, c + 7, r)
                        split_low(dve, c + 8, r)
                        t_low(r + 1)
                        split_low(dve, c + 9, r)
                        mult(r + 2, r * RAW + (MOE0 + 8))
                        split_low(dve, c + 10, r)
                        split_low(dve, c + 11, r)
                    t_low(j * EXP_BLOCKS + EXP_BLOCKS)
                add_rows(njobs * 4)

            dve.wait_ge(s["const_in"], 32)
            dve.wait_ge(s["x_in"], 16)
            for l in range(DEPTH):
                dve.wait_ge(s["wf_high"], 2 * l + 2)
                nc.vector.tensor_tensor(wfL[:], A(l, A_WF, 128), wfH[:].bitcast(F32), ALU.subtract).then_inc(s["wf_low"], 1)
                mixer(l)
                dense() if l == 0 else experts()

        @block.tensor
        def _(pe):
            def norm(nn):
                for g in range(2):
                    pe.wait_ge(s["squares"], 2 * nn + g + 1)
                    for k in range(4 * g, 4 * g + 4):
                        ins = pe.matmul(bank[3][:, 0:S], C(C_ONES), hf[:, k, :], start=k == 0, stop=k == KC - 1)
                ins.then_inc(s["norm_stats"], 1)

            def small_h(dst, at, l):
                for t in range(TT):
                    ins = products(pe, dst[:, 8 * t:8 * t + 8], [
                        (hH[:, k, t * P:t * P + P], hL[:, k, t * P:t * P + P],
                         wfH[:, at + 8 * k:at + 8 * k + 8], wfL[:, at + 8 * k:at + 8 * k + 8]) for k in range(KC)])
                return ins

            def bank_free(l, u):
                if u >= 3:
                    who, name = (ACT_UNITS, "unit_used_act") if u - 3 in ACT_UNITS else (DVE_UNITS, "unit_used_dve")
                    pe.wait_ge(s[name], len(who) * l + who.index(u - 3) + 1)

            def channel_unit(l, u, H, L, act_h, act_l, columns):
                bank_free(l, u)
                K = H.shape[1]
                for m in range(2):
                    c0 = columns + m * P
                    ins = products(pe, bank[u % 3][:, m * S:m * S + S], [
                        (H[:, k, c0:c0 + P], L[:, k, c0:c0 + P], act_h[:, k, :], act_l[:, k, :]) for k in range(K)])
                ins.then_inc(s["used" if UNIT_LAST[u] else "unit_part"], 1)

            def mixer(l):
                b = BASE[l]
                norm(2 * l)
                pe.wait_ge(s["wf_low"], l + 1)
                pe.wait_ge(s["h_low_done"], 8 * l + 4)
                small_h(bank[3][:, 256:272], 0, l).then_inc(s["f_logits"], 1)

                def q_k_stats(u):
                    pe.wait_ge(s["qk_sq"], 4 * l + u - 1)
                    pe.matmul(bank[6 + u % 2][:], C(C_HALVES), qsq[:, u % 2, :], start=True, stop=True).then_inc(s["qk_stats"], 1)

                def pool_means():
                    pe.wait_ge(s["unit_used_act"], len(ACT_UNITS) * l + 4)
                    pe.wait_ge(s["f_soft"], 2 * l + 2)
                    for c in range(2):
                        for g in range(2):
                            w = C_POOL + 3 * (2 * c + g)
                            lo = 128 * c + 64 * g
                            pe.matmul(bank[3][64 * g:64 * g + 64, c * S:c * S + S], pt_[:, 0, lo:lo + 64], C(w, 2),
                                      start=True, stop=False)
                            ins = pe.matmul(bank[3][64 * g:64 * g + 64, c * S + P:c * S + S], pt_[:, 1, lo:lo + 64], C(w + 2),
                                            start=False, stop=True)
                    ins.then_inc(s["pooled_ready"], 1)

                def pool_map():
                    pe.wait_ge(s["pool_in_ready"], l + 1)
                    for c in range(2):
                        ins = pe.matmul(bank[3][:, c * S:c * S + S], A(l, A_POOLW + P * c, P), pooled[:, c, :], start=True, stop=True)
                    ins.then_inc(s["pool_lin"], 1)

                def ln_sum(src, at, name):
                    for c in range(CONVC):
                        ins = pe.matmul(bank[3][:, at:at + S], C(C_ONES), src[:, c, :], start=c == 0, stop=c == 1)
                    ins.then_inc(s[name], 1)

                def head_scores(h):
                    pe.wait_ge(s["decays"], 3 * (8 * l + h) + 3)
                    if h >= 2:
                        pe.wait_ge(s["exp_done"], 2 * (8 * l + h - 2) + 2)
                    B = bank[4 + h % 2]
                    rows = slice(64 * (h % 2), 64 * (h % 2) + 64)
                    q, k = qk[rows, h // 2, :], qk[rows, 4 + h // 2, :]
                    pe.matmul(B[:, 0:128], q[:, 0:P], k[:, 0:P], start=True, stop=False)
                    pe.matmul(B[:, 0:128], decay[:, h % 2, 0, :], C(C_AFTER), start=False, stop=False)
                    pe.matmul(B[:, 0:128], ident, C(C_MASK), start=False, stop=True)
                    pe.matmul(B[:, 128:384], q[:, P:S], k, start=True, stop=False)
                    pe.matmul(B[:, 128:256], decay[:, h % 2, 2, :], C(C_AFTER), start=False, stop=False)
                    pe.matmul(B[:, 128:384], decay[:, h % 2, 1, :], C(C_ONES, 2), start=False, stop=False)
                    pe.matmul(B[:, 256:384], ident, C(C_MASK), start=False, stop=True).then_inc(s["scores"], 1)

                def head_turn(h):
                    pe.wait_ge(s["prob_done"], 2 * (8 * l + h) + 2)
                    if h >= 1:
                        pe.wait_ge(s["prob_t_out"], 8 * l + h)
                    for t in range(3):
                        ins = pe.transpose(bank[6][:, t * P:t * P + P], prob[:, h % 2, t * P:t * P + P], ident)
                    ins.then_inc(s["prob_t"], 1)

                def head_values(h):
                    pe.wait_ge(s["prob_t_out"], 8 * l + h + 1)
                    if h >= 2 and h % 2 == 0:
                        pe.wait_ge(s["y_low_done"], 6 * l + LOW_ORDER[4 + h // 2 - 1])
                    rows = slice(64 * (h % 2), 64 * (h % 2) + 64)
                    v = slice(HD * h, HD * h + HD)
                    pe.matmul(bank[7][rows, 0:S], vt[:, 0, v], probT[:, 0:S], start=True, stop=False)
                    pe.matmul(bank[7][rows, P:S], vt[:, 1, v], probT[:, S:S + P], start=False,
                              stop=True).then_inc(s["pv"], 1)

                for n in range(P_BRPOOL):
                    H, L = take_piece(pe, b + n)
                    if n in (P_V, P_V + 1, P_POOL):
                        bank_free(l, n)
                        for t in range(TT):
                            ins = products(pe, bank[n % 3][:, t * 256:t * 256 + 256], [
                                (hH[:, k, t * P:t * P + P], hL[:, k, t * P:t * P + P], H[:, k, :], L[:, k, :])
                                for k in range(KC)])
                        ins.then_inc(s["used"], 1)
                    else:
                        channel_unit(l, n, H, L, hH, hL, 0)
                    if 3 <= n <= 6:
                        q_k_stats(n - 1)
                    if n == 9:
                        pool_means()
                    if n == 10:
                        pool_map()
                    if n == 15:
                        pe.wait_ge(s["y_full"], 2 * l + 1)
                        pe.wait_ge(s["ln_taps"], 2 * l + 2)
                        ln_sum(cv, 0, "ln_mean")
                    if n == 18:
                        pe.wait_ge(s["ln_sq"], l + 1)
                        ln_sum(cs, S, "ln_var")
                    if 10 <= n <= 17:
                        head_scores(n - 10)
                    if 12 <= n <= 19:
                        head_turn(n - 12)
                    if 13 <= n <= 20:
                        head_values(n - 13)
                u = 21
                for n in range(P_BRPOOL, P_OUT):
                    first, K, units = {P_BRPOOL: (0, 2, 4), P_BRCONV: (2, 2, 4), P_BRATTN: (4, 4, 2), P_BRATTN + 1: (4, 4, 2)}[n]
                    need = {P_BRPOOL: LOW_ORDER[0], P_BRCONV: LOW_ORDER[2], P_BRATTN: 6, P_BRATTN + 1: 6}[n]
                    pe.wait_ge(s["y_low_done"], 6 * l + need)
                    H, L = take_piece(pe, b + n, 0, K)
                    for m in range(units):
                        channel_unit(l, u, H, L, yH[:, first:first + K, :], yL[:, first:first + K, :], 256 * m)
                        u += 1
                pe.wait_ge(s["merged_low"], 4 * l + 4)
                for n in range(P_OUT, MIX_PIECES):
                    H, L = take_piece(pe, b + n)
                    channel_unit(l, u, H, L, hH, hL, 0)
                    u += 1

            def zero_bank(b):
                return pe.matmul(bank[b][:], zero[:, 0:P], zero[:], start=True, stop=False)

            def dense():
                norm(1)
                pe.wait_ge(s["h_low_done"], 8)
                pe.wait_ge(s["zeros"], 1)
                for m in range(4):
                    zero_bank(4 + m)

                def up(c, r, b):
                    H, L = take_piece(pe, c, r)
                    for m in range(2):
                        ins = products(pe, bank[b][:, m * S:m * S + S], [
                            (H[:, k, m * P:m * P + P], L[:, k, m * P:m * P + P], hH[:, k, :], hL[:, k, :]) for k in range(KC)])
                    ins.then_inc(s["used"], 1)

                def down(c, r, count, stop=False):
                    H, L = take_piece(pe, c, r, 2)
                    pe.wait_ge(s["d_low"], count)
                    for m in range(KC):
                        ins = products(pe, bank[4 + m // 2][:, (m % 2) * S:(m % 2) * S + S], [
                            (H[:, k, m * P:m * P + P], L[:, k, m * P:m * P + P],
                             gH[:, k * S:k * S + S], gL[:, k * S:k * S + S]) for k in range(2)], start=False, stop=stop and m % 2 == 1)
                    ins.then_inc(s["used"], 1)

                up(DENSE0, 0, 0)
                up(DENSE0 + 1, 0, 2)
                with pe.Fori(0, (DENSE_BLOCKS - 1) // 2) as i:
                    for u in range(2):
                        c = DENSE0 + 2 + 3 * u
                        up(c, i, 1 - u)
                        up(c + 1, i, 3 - u)
                        down(c + 2, i, i * 2 + (u + 1))
                down(DENSE0 + DENSE_PIECES - 1, 0, DENSE_BLOCKS, stop=True)

            def experts():
                norm(3)
                pe.wait_ge(s["h_low_done"], 16)
                small_h(bank[7][:, 0:16], 64, 1).then_inc(s["r_logits"], 1)
                for f in range(12):
                    src = (hH, hL, xT)[f // 4]
                    if f >= 7:
                        pe.wait_ge(s["fill_act"], f - 6)
                    t, half_ = f % 4 // 2, f % 2
                    for k in range(4):
                        a = src[:, 4 * half_ + k, t * P:t * P + P]
                        ins = pe.transpose(bank[f % 7][:, k * P:k * P + P], a if f >= 8 else a.bitcast(F32), ident)
                    ins.then_inc(s["fill"], 1)
                pe.wait_ge(s["r_pick"], 1)
                sel = [jobs[:, 0, t, 0:8] for t in range(TT)]
                pe.matmul(bank[7][:, 32:40], C(C_BEFORE), sel[0], start=True, stop=True)
                pe.matmul(bank[7][:, 40:48], C(C_ONES), sel[0], start=True, stop=False)
                pe.matmul(bank[7][:, 40:48], C(C_BEFORE), sel[1], start=False, stop=True)
                pe.matmul(bank[7][:, 64:72], C(C_ONES), sel[0], start=True, stop=False)
                pe.matmul(bank[7][:, 64:72], C(C_ONES), sel[1], start=False, stop=True).then_inc(s["r_rank"], 1)

                def gather(g):
                    src = htH if g < 2 else htL
                    for k in range(4):
                        ch = 4 * (g % 2) + k
                        for t in range(TT):
                            ins = pe.matmul(bank[(5, 6, 7, 5)[g]][:, k * P:k * P + P], src[:, t, ch * P:ch * P + P],
                                            perm[:, t, :], start=t == 0, stop=t == TT - 1)
                    ins.then_inc(s["m_gather"], 1)

                def up(c, r, b):
                    for half_ in range(2):
                        H, L = take_piece(pe, c + half_, r, 4)
                        ins = products(pe, bank[b][:], [
                            (hgH[:, 4 * half_ + k, :], hgL[:, 4 * half_ + k, :], H[:, k, :], L[:, k, :]) for k in range(4)],
                            start=half_ == 0, stop=half_ == 1)
                        ins.then_inc(s["used"], 1)

                def turn(count):
                    pe.wait_ge(s["m_mult"], count)
                    for k in range(4):
                        ins = pe.transpose(bank[4][:, k * P:k * P + P], gu[:, k * P:k * P + P], ident)
                    ins.then_inc(s["m_t"], 1)

                def down(c, r, count, between=None):
                    pe.wait_ge(s["m_low"], count)
                    for half_ in range(2):
                        H, L = take_piece(pe, c + half_, r, 2)
                        for n in range(2):
                            ins = products(pe, bank[2 + n][:], [
                                (gH[:, (2 * half_ + k) * P:(2 * half_ + k) * P + P], gL[:, (2 * half_ + k) * P:(2 * half_ + k) * P + P],
                                 H[:, k, 512 * n:512 * n + 512], L[:, k, 512 * n:512 * n + 512]) for k in range(2)],
                                start=False, stop=between is not None and half_ == 1)
                        ins.then_inc(s["used"], 1)
                        if half_ == 0 and between is not None:
                            between()

                def combine(count):
                    for q, b in enumerate((4, 7, 5, 6)):
                        ins = pe.matmul(bank[b][:], permT[:, (q // 2) * P:(q // 2) * P + P],
                                        ysb[:, 512 * (q % 2):512 * (q % 2) + 512], start=True, stop=True)
                        ins.then_inc(s["m_comb"], 1)

                pe.wait_ge(s["m_perm"], 2)
                pe.wait_ge(s["zeros"], 2)
                pe.wait_ge(s["fill_act"], 8)
                pe.wait_ge(s["fill_dve"], 4)
                for n in range(2):
                    ins = pe.matmul(bank[2 + n][:], zero[:, 0:P], zero[:], start=True, stop=True)
                ins.then_inc(s["m_zero"], 1)
                for g in range(4):
                    if g == 3:
                        pe.wait_ge(s["m_gout"], 1)
                    gather(g)
                pe.wait_ge(s["jobs_ready"], 1)
                njobs = pe.value_load(jobi[0:1, 12:13], min_val=EXPERTS, max_val=EXPERTS + EXTRA_JOBS)
                with pe.Fori(0, njobs) as j:
                    r0, c = j * EXP_BLOCKS, MOE0

                    def last_between():
                        pe.wait_ge(s["m_gout"], j * 4 + 5)
                        gather(3)
                        pe.wait_ge(s["m_gout"], j * 4 + 6)
                        for t in range(TT):
                            ins = pe.transpose(bank[6][:, t * P:t * P + P], permG[:, t, :], ident)
                        ins.then_inc(s["m_permt"], 1)

                    pe.wait_ge(s["m_gout"], j * 4 + 4)
                    up(c, r0, 0)
                    up(c + 2, r0, 1)
                    pe.wait_ge(s["m_yout"], j * 2 + 2)
                    pe.wait_ge(s["m_ptout"], j + 1)
                    combine(j * 4)
                    zero_bank(2)
                    zero_bank(3)
                    with pe.Fori(0, EXP_BLOCKS - 1) as i:
                        r = j * EXP_BLOCKS + i
                        pe.wait_ge(s["m_silu"], r + 1)
                        up(c + 4, r, 0)
                        pe.wait_ge(s["m_add"], j * 4 + 4)
                        turn(r + 1)
                        up(c + 6, r, 1)
                        down(c + 8, r, r + 1)
                    pe.wait_ge(s["m_perm"], j * 4 + 6)
                    for g in range(3):
                        gather(g)
                    turn(j * EXP_BLOCKS + EXP_BLOCKS)
                    down(c + JOB_PIECES - 2, r0, j * EXP_BLOCKS + EXP_BLOCKS, between=last_between)
                pe.wait_ge(s["m_yout"], njobs * 2 + 2)
                pe.wait_ge(s["m_ptout"], njobs + 1)
                combine(njobs * 4)

            pe.wait_ge(s["const_in"], 32)
            for l in range(DEPTH):
                mixer(l)
                dense() if l == 0 else experts()


def constants():
    row, col = np.arange(P)[:, None], np.arange(P)[None, :]
    blocks = [row == col, row // HD == col // HD, row <= col, np.ones((P, P)), row > col, row < col,
              np.where(col > row, NEG, 0.0), np.broadcast_to(col, (P, P))]
    for w in WINDOWS:
        lag = col - row
        seen = np.minimum(col + 1, w)
        blocks.append(((lag >= 0) & (lag < w)) / seen - (lag == 0))
        blocks.append((lag + P < w) / float(w) + 0.0 * col)
        blocks.append(((lag >= 0) & (lag < w)) / float(w) - (lag == 0))
    return np.ascontiguousarray(np.stack([np.asarray(b, np.float32) for b in blocks], 1))


def channels(a):
    return np.asarray(a).reshape(-1, P).T


def layer_params(i, l):
    out = np.zeros((P, N_PARAM), np.float32)

    def put(at, a):
        out[:, at:at + a.shape[1]] = a

    put(A_GMIX, channels(i["g_mix"][l]))
    put(A_GFFN, channels(i["g_ffn"][l]))
    put(A_BGATE, channels(i["b_gate"][l]))
    put(A_PSCALE, channels(i["pool_scale"][l]))
    for c in range(CONVC):
        put(A_CONVW + c * TAPS, np.asarray(i["conv_w"][l])[:, c * P:c * P + P].T)
    put(A_CONVB, channels(i["conv_b"][l]))
    put(A_LNG, channels(i["conv_ln_g"][l]))
    put(A_LNB, channels(i["conv_ln_b"][l]))
    put(A_QG, np.concatenate([i["q_norm_g"][l]] * 2)[:, None])
    put(A_KG, np.concatenate([i["k_norm_g"][l]] * 2)[:, None])
    put(A_BF, np.broadcast_to(np.asarray(i["b_forget"][l])[None, :], (P, HEADS)))
    out[:, A_EPS] = EPS
    out[:, A_EPS64] = EPS * HD
    for g in range(4):
        lo, at = HD * (g % 2), A_POOLW + P * (g // 2) + HD * (g % 2)
        out[lo:lo + HD, at:at + HD] = i["pool_w"][l][g]
    put(A_WF, np.asarray(i["w_in"][l])[:, OFF_F:OFF_G].reshape(KC, P, HEADS).transpose(1, 0, 2).reshape(P, -1))
    if l % 2:
        put(A_ROUTER, np.asarray(i["router_w"][l // 2]).reshape(KC, P, EXPERTS).transpose(1, 0, 2).reshape(P, -1))
    return out


def kernel(**inputs):
    import concourse.bacc as bacc
    from concourse.bass_utils import run_bass_kernel_spmd

    i = {k: np.asarray(v) for k, v in inputs.items()}
    arrays = {
        "xt": np.ascontiguousarray(i["x"][0].T.reshape(KC, P, S).transpose(1, 0, 2)),
        "consts": constants(),
        "params": np.ascontiguousarray(np.stack([layer_params(i, l) for l in range(DEPTH)], 1)),
    }
    for name in ("w_in", "w_br_pool", "w_br_conv", "w_br_attn", "w_out", "ffn_w1", "ffn_w3", "ffn_w2",
                 "exp_w1", "exp_w3", "exp_w2"):
        arrays[name] = np.ascontiguousarray(i[name])
    nc = bacc.Bacc("TRN2", target_bir_lowering=False, num_devices=1)
    aps = [nc.dram_tensor(n, a.shape, mybir.dt.from_np(a.dtype), kind="ExternalInput").ap() for n, a in arrays.items()]
    out = nc.dram_tensor("out", (1, S, D), F32, kind="ExternalOutput").ap()
    trunk(nc, *aps, out)
    return run_bass_kernel_spmd(nc, [arrays], core_ids=[0]).results[0]["out"]
```

```python
from contextlib import ExitStack

import numpy as np

import concourse.bass as bass
from concourse import mybir

F32 = mybir.dt.float32
F32R = mybir.dt.float32r
I32 = mybir.dt.int32
U32 = mybir.dt.uint32
ALU = mybir.AluOpType
ACT = mybir.ActivationFunctionType
AX_X = mybir.AxisListType.X

P = 128
D = 1024
KC = D // P
S = 256
TT = S // P
DEPTH = 2
HEADS = 8
HD = 64
WINDOWS = (2, 4, 8, 16)
TAPS = 31
PAD = TAPS - 1
CONVC = 2
OFF_POOL, OFF_CONV, OFF_Q, OFF_K, OFF_V, OFF_F, OFF_G = 0, 256, 768, 1280, 1792, 2304, 2312
D_FF = 2816
D_EXP = 3584
EXPERTS = 8
EXTRA_JOBS = 3
EPS = 1e-6
NEG = -1e30

RAW = 6
SPLIT = 3
PIECE = 2048

C_IDENT, C_HALVES, C_UPTO, C_ONES, C_AFTER, C_BEFORE, C_MASK, C_IOTA, C_POOL = range(9)
N_CONST = C_POOL + 3 * len(WINDOWS)

A_GMIX, A_GFFN, A_BGATE, A_PSCALE, A_CONVW, A_CONVB, A_LNG, A_LNB, A_QG, A_KG, A_BF = (
    0, 8, 16, 40, 42, 104, 106, 108, 110, 111, 112)
A_EPS, A_EPS64, A_POOLW, A_WF, A_ROUTER = 120, 121, 122, 378, 442
N_PARAM = A_ROUTER + 56 + P

SMALL = 2 * KC * 8 - 8 + P

P_CONV, P_Q, P_K, P_V, P_POOL, P_GATE, P_BRPOOL, P_BRCONV, P_BRATTN, P_OUT = 0, 2, 4, 6, 8, 9, 21, 22, 23, 25
MIX_PIECES = 29
DENSE_BLOCKS = D_FF // S
DENSE_PIECES = 3 * DENSE_BLOCKS
EXP_BLOCKS = D_EXP // 512
JOB_PIECES = 6 * EXP_BLOCKS
BASE = [0, MIX_PIECES + DENSE_PIECES]
DENSE0 = MIX_PIECES
MOE0 = BASE[1] + MIX_PIECES

UNITS = 37
ACT_UNITS = [1, 6, 7, 8] + list(range(9, 21))
DVE_UNITS = [0, 2, 3, 4, 5] + list(range(21, 37))
UNIT_PIECE = list(range(21)) + [21] * 4 + [22] * 4 + [23] * 2 + [24] * 2 + list(range(25, 29))
UNIT_BANK = [0, 1, 2, 4, 5, 0, 1, 2, 5] + [u % 3 for u in range(9, UNITS)]
UNIT_BEFORE = [max((v for v in range(u) if UNIT_BANK[v] == UNIT_BANK[u]), default=None) for u in range(UNITS)]
UNIT_LAST = [u + 1 == UNITS or UNIT_PIECE[u + 1] != UNIT_PIECE[u] for u in range(UNITS)]
PARTS = UNIT_LAST.count(False)
GATHER_BANKS = (5, 6, 7, 0)
TAPS_AT = {4: 6, 5: 6, 6: 1, 7: 1, 8: 1, 9: 1, 10: 8, 11: 8, 12: 8, 13: 8, 14: 7, 15: 7}
HIGH_ORDER = {0: 1, 4: 2, 5: 3, 6: 4, 7: 5, 2: 6}
LOW_ORDER = {0: 1, 4: 2, 5: 3, 6: 4, 2: 5, 7: 6}


def pieces_of_mixer(l, w_in, w_br_pool, w_br_conv, w_br_attn, w_out):
    win = w_in[l].rearrange("(k p) n -> p k n", p=P)
    wout = w_out[l].rearrange("(k p) n -> p k n", p=P)
    attn = w_br_attn[l].rearrange("(k p) n -> p k n", p=P)
    columns = [OFF_CONV, OFF_CONV + 256, OFF_Q, OFF_Q + 256, OFF_K, OFF_K + 256, OFF_V, OFF_V + 256, OFF_POOL]
    columns += [OFF_G + 256 * i for i in range(12)]
    out = [(win[:, :, c:c + 256], KC) for c in columns]
    out += [(w_br_pool[l].rearrange("(k p) n -> p k n", p=P), 2), (w_br_conv[l].rearrange("(k p) n -> p k n", p=P), 2)]
    out += [(attn[:, :, 512 * i:512 * i + 512], 4) for i in range(2)]
    out += [(wout[:, :, 256 * i:256 * i + 256], KC) for i in range(4)]
    assert len(out) == MIX_PIECES
    return out


def trunk(nc, xt, consts, params, w_in, w_br_pool, w_br_conv, w_br_attn, w_out,
          ffn_w1, ffn_w3, ffn_w2, exp_w1, exp_w3, exp_w2, out):
    with ExitStack() as ctx:
        def sb(name, shape, dt=F32):
            return ctx.enter_context(nc.sbuf_tensor(name, shape, dt))

        def sem(name):
            return ctx.enter_context(nc.semaphore(name))

        bank = [ctx.enter_context(nc.psum_tensor(f"bank{i}", [P, 512], F32)) for i in range(8)]

        raw = [sb(f"raw{i}", [P, PIECE]) for i in range(RAW)]
        wh = [sb(f"w_high{i}", [P, PIECE], F32R) for i in range(SPLIT)]
        wl = [sb(f"w_low{i}", [P, PIECE], F32R) for i in range(SPLIT)]
        xT = sb("xT", [P, KC, S])
        hf = sb("h_full", [P, KC, S])
        hH = sb("h_high", [P, KC, S], F32R)
        hL = sb("h_low", [P, KC, S], F32R)
        cst = sb("cst", [P, N_CONST, P])
        par = sb("par", [P, DEPTH, N_PARAM])
        rt = sb("rt", [P, 512])
        rinv = sb("rinv", [P, 512])
        wfH = sb("wf_high", [P, SMALL], F32R)
        wfL = sb("wf_low", [P, SMALL], F32R)
        ones = sb("ones", [P, P])
        warm = sb("warm", [P, 1])

        f8 = rinv[0:8, S:2 * S]

        with ExitStack() as mix:
            def mb(name, shape, dt=F32):
                return mix.enter_context(nc.sbuf_tensor(name, shape, dt))

            fg = mb("fg", [P, 6, TT * HEADS])
            half = mb("half_bias", [P, 24])
            gate = mb("gate", [P, 24, S])
            zp = mb("zp", [P, CONVC, PAD + S])
            cv = mb("cv", [P, CONVC, S])
            cs = mb("cs", [P, CONVC, S])
            vt = mb("vt", [P, TT, 512])
            decay = mb("decay", [P, 2, 3, P])
            negmax = mb("negmax", [P, 2, 2])
            psum_ = mb("prob_sum", [P, 2, 2])
            pinv = mb("prob_inv", [P, 2, 2])
            prob = mb("prob", [P, 2, 384])
            probT = mb("probT", [P, 384])
            yH = mb("y_high", [P, 8, S], F32R)
            yL = mb("y_low", [P, 8, S], F32R)
        yf = cs
        attn = rt[:, S:2 * S], rinv[:, S:2 * S]
        qk = hf
        qsq = gate[:, 20:24, :].rearrange("p a b -> p (a b)").rearrange("p (u n) -> p u n", u=2)
        pt_ = gate[:, 18:20, :]
        pooled = gate[:, 16:18, :]

        zero = sb("zero", [P, 512], F32R)
        sl = sb("sl", [P, 512])
        gu = sb("gu", [P, 512])
        gH = sb("g_high", [P, 512], F32R)
        gL = sb("g_low", [P, 512], F32R)
        htH = sb("ht_high", [P, TT, D], F32R)
        htL = sb("ht_low", [P, TT, D], F32R)
        hgH = sb("hg_high", [P, KC, P], F32R)
        hgL = sb("hg_low", [P, KC, P], F32R)
        xacc = sb("xacc", [P, TT, D])
        ysb = sb("ysb", [P, D])
        permG = sb("perm_gated", [P, TT, P])
        permT = sb("perm_t", [P, S])
        perm = sb("perm", [P, TT, P], F32R)
        lg = sb("lg", [P, TT, 8])
        top = sb("top", [P, TT, 8])
        topi = sb("topi", [P, TT, 8], U32)
        topf = sb("topf", [P, TT, 8])
        wt = sb("wt", [P, 4, TT])
        pick = sb("pick", [P, 2, TT, 8])
        tmp8 = sb("tmp8", [P, TT, 8])
        cnt = sb("cnt", [P, 6, 8])
        over = sb("over", [P, EXTRA_JOBS, 8])
        jobs = sb("jobs", [P, 3, TT, 12])
        jobf = sb("jobf", [P, 16])
        jobi = sb("jobi", [P, 16], I32)

        names = """const_in high_done split_done used
            squares norm_stats norm_root norm_h h_high_done h_low_done norm_step
            f_logits f_soft decay_in decays unit_part ln_taps unit_used_act unit_used_dve
            qk_sq qk_stats qk_root pool_in_ready pooled_ready pool_lin
            y_full y_high_done y_low_done ln_mean ln_zc ln_sq ln_var ln_root ln_v ln_th
            scores max_done exp_done prob_done prob_t prob_t_out pv values_copied merged merged_high merged_low
            dve_step act_step wf_high wf_low zeros par_in tables ones_set f_raw f_copied d_y
            d_silu d_mult d_high d_low d_res
            r_logits r_lg r_exp r_pick r_rank fill fill_act
            m_zero m_silu m_mult m_t m_high m_low m_yout m_gather m_gout m_perm m_permt m_ptout
            m_comb m_add jobs_ready stored""".split()
        s = {n: sem(n) for n in names}
        x_in = [sem(f"x_in{m}") for m in range(4)]
        raw_in = [sem(f"raw_in{i}") for i in range(RAW)]

        def C(i, n=1):
            return cst[:, i:i + n, :].rearrange("p a b -> p (a b)")

        def A(l, i, n=1):
            return par[:, l, i:i + n]

        ident = C(C_IDENT)

        def fold(ap, k):
            return ap.rearrange("p (k n) -> p k n", k=k)

        def num(c, r):
            return c if isinstance(r, int) and r == 0 else r * RAW + c

        def unit_ready(eng, l, u):
            if UNIT_LAST[u]:
                eng.wait_ge(s["used"], BASE[l] + UNIT_PIECE[u] + 1)
            else:
                eng.wait_ge(s["unit_part"], PARTS * l + UNIT_LAST[:u + 1].count(False))

        def x_ready(eng, nn, m):
            if nn == 0:
                eng.wait_ge(x_in[m], 16)
            elif nn == 2:
                eng.wait_ge(s["d_res"], m + 1)
            else:
                eng.wait_ge(s["unit_used_dve"], len(DVE_UNITS) * (nn // 2) + DVE_UNITS.index(33 + m) + 1)

        def load_piece(sp, c, r, src, k):
            if not (isinstance(r, int) and c < RAW):
                sp.wait_ge(s["split_done"], num(c - RAW + 1, r))
            sp.dma_start(fold(raw[c % RAW][:], k), src).then_inc(raw_in[c % RAW], 16)

        def split_high(act, c, r=0):
            act.wait_ge(raw_in[c % RAW], 16 * (c // RAW + 1) if isinstance(r, int) else r * 16 + 16 * (c // RAW + 1))
            if not (isinstance(r, int) and c < SPLIT):
                act.wait_ge(s["used"], num(c - SPLIT + 1, r))
            nc.scalar.activation(wh[c % SPLIT][:], raw[c % RAW][:], ACT.Copy).then_inc(s["high_done"], 1)

        def split_low(dve, c, r=0):
            dve.wait_ge(s["high_done"], num(c + 1, r))
            nc.vector.tensor_tensor(wl[c % SPLIT][:], raw[c % RAW][:], wh[c % SPLIT][:].bitcast(F32),
                                    ALU.subtract).then_inc(s["split_done"], 1)

        def take_piece(pe, c, r=0, k=KC):
            pe.wait_ge(s["split_done"], num(c + 1, r))
            return fold(wh[c % SPLIT][:], k), fold(wl[c % SPLIT][:], k)

        def products(pe, dst, terms, start=True, stop=True):
            for i, (lh, ll, rh, rl) in enumerate(terms):
                pe.matmul(dst, lh, rh, start=start and i == 0, stop=False)
                pe.matmul(dst, lh, rl, start=False, stop=False)
                last = pe.matmul(dst, ll, rh, start=False, stop=stop and i == len(terms) - 1)
            return last

        block = ctx.enter_context(nc.Block())

        @block.sync
        def _(sp):
            for m in range(4):
                sp.dma_start(xT[:, 2 * m:2 * m + 2, :], xt[:, 2 * m:2 * m + 2, :]).then_inc(x_in[m], 16)
            sp.dma_start(par[:], params).then_inc(s["par_in"], 16)
            d1 = ffn_w1[0].rearrange("(k p) n -> p k n", p=P)
            d3 = ffn_w3[0].rearrange("(k p) n -> p k n", p=P)
            d2 = ffn_w2[0].rearrange("(b k p) n -> b p k n", p=P, k=2)
            for l in range(DEPTH):
                for n, (src, k) in enumerate(pieces_of_mixer(l, w_in, w_br_pool, w_br_conv, w_br_attn, w_out)):
                    load_piece(sp, BASE[l] + n, 0, src, k)
                    if l == 0 and n == 1:
                        sp.dma_start(cst[:], consts).then_inc(s["const_in"], 16)
                if l == 0:
                    load_piece(sp, DENSE0, 0, d1[:, :, 0:S], KC)
                    load_piece(sp, DENSE0 + 1, 0, d3[:, :, 0:S], KC)
                    with sp.Fori(0, (DENSE_BLOCKS - 1) // 2) as i:
                        for u in range(2):
                            c = DENSE0 + 2 + 3 * u
                            at = bass.ds(i * (2 * S) + (u + 1) * S, S)
                            load_piece(sp, c, i, d1[:, :, at], KC)
                            load_piece(sp, c + 1, i, d3[:, :, at], KC)
                            load_piece(sp, c + 2, i, d2[bass.ds(i * 2 + u, 1)].rearrange("b p k n -> (b p) k n"), 2)
                    load_piece(sp, DENSE0 + DENSE_PIECES - 1, 0, d2[DENSE_BLOCKS - 1], 2)
            e1 = exp_w1[0].rearrange("e (k p) n -> e p k n", p=P)
            e3 = exp_w3[0].rearrange("e (k p) n -> e p k n", p=P)
            e2 = exp_w2[0].rearrange("e (b k p) n -> e b p k n", p=P, k=2)

            def job(j, e):
                one = bass.ds(e, 1)

                def up(c, r, fb):
                    for w, k0 in ((e1, 0), (e1, 4), (e3, 0), (e3, 4)):
                        load_piece(sp, c, r, w[one, :, k0:k0 + 4, fb].rearrange("e p k n -> (e p) k n"), 4)
                        c += 1

                def down(c, r, b):
                    for u in range(2):
                        load_piece(sp, c + u, r, e2[one, bass.ds(b + u, 1)].rearrange("e b p k n -> (e b p) k n"), 2)

                up(MOE0, j * EXP_BLOCKS, bass.ds(0, 512))
                with sp.Fori(0, EXP_BLOCKS - 1) as i:
                    r = j * EXP_BLOCKS + i
                    up(MOE0 + 4, r, bass.ds(i * 512 + 512, 512))
                    down(MOE0 + 8, r, i * 2)
                down(MOE0 + JOB_PIECES - 2, j * EXP_BLOCKS, 2 * (EXP_BLOCKS - 1))

            job(0, 0)
            sp.wait_ge(s["jobs_ready"], 1)
            njobs = sp.value_load(jobi[0:1, 12:13], min_val=EXPERTS, max_val=EXPERTS + EXTRA_JOBS)
            with sp.Fori(1, njobs) as j:
                job(j, sp.value_load(jobi[0:1, bass.ds(j, 1)], min_val=0, max_val=EXPERTS - 1))
            for q in range(4):
                sp.wait_ge(s["m_add"], njobs * 4 + (q + 1))
                t, c = q // 2, 512 * (q % 2)
                sp.dma_start(out[0, t * P:t * P + P, c:c + 512], xacc[:, t, c:c + 512]).then_inc(s["stored"], 16)
            sp.wait_ge(s["stored"], 64)

        @block.gpsimd
        def _(pool):
            for l in range(DEPTH):
                lf = fg[:, 5, :].rearrange("p (t h) -> p t h", t=TT)
                pool.wait_ge(s["decay_in"], l + 1)
                for h in range(HEADS):
                    if h >= 2:
                        pool.wait_ge(s["scores"], 8 * l + h - 1)
                    for k, (m, tile) in enumerate(((C_UPTO, 0), (C_UPTO, 1), (C_ONES, 0))):
                        nc.gpsimd.tensor_scalar(decay[:, h % 2, k, :], C(m), lf[:, tile, h:h + 1], None,
                                                ALU.mult).then_inc(s["decays"], 1)

        @block.scalar
        def _(act):
            def squares(nn, m):
                if m == 0:
                    nc.scalar.activation(warm[:], warm[:], ACT.Sqrt)
                x_ready(act, nn, m)
                nc.scalar.activation(hf[:, 2 * m:2 * m + 2, :], xT[:, 2 * m:2 * m + 2, :],
                                     ACT.Square).then_inc(s["squares"], 1)

            def norm(nn, ahead=()):
                act.wait_ge(s["norm_stats"], nn + 1)
                nc.scalar.activation(rt[:, 0:S], bank[3][:, 0:S], ACT.Sqrt, bias=A(0, A_EPS),
                                     scale=1.0 / D).then_inc(s["norm_root"], 1)
                for c in ahead[:1]:
                    split_high(act, c)
                for g in range(4):
                    act.wait_ge(s["norm_h"], 8 * nn + 2 * g + 2)
                    nc.scalar.activation(hH[:, 2 * g:2 * g + 2, :], hf[:, 2 * g:2 * g + 2, :],
                                         ACT.Copy).then_inc(s["h_high_done"], 1)
                for c in ahead[1:]:
                    split_high(act, c)

            def mixer(l):
                b = BASE[l]
                norm(2 * l, [0, 1] if l == 0 else [])
                split_high(act, b + 2)
                if l == 0:
                    act.wait_ge(s["const_in"], 16)
                act.wait_ge(s["f_soft"], 2 * l + 1)
                nc.scalar.activation(fg[:, 2, :], fg[:, 1, :], ACT.Exp, scale=-1.0).then_inc(s["act_step"], 1)
                act.wait_ge(s["act_step"], 2 * l + 1)
                nc.scalar.activation(fg[:, 3, :], fg[:, 2, :], ACT.Ln, bias=C(C_ONES)[:, 0:1]).then_inc(s["act_step"], 1)

                def gate_out(u):
                    unit_ready(act, l, u)
                    for m in range(2):
                        g = 2 * (u - P_GATE) + m
                        ins = nc.scalar.activation(gate[:, g, :], bank[UNIT_BANK[u]][:, m * S:m * S + S], ACT.Tanh,
                                                   bias=half[:, g:g + 1], scale=0.5)
                    ins.then_inc(s["unit_used_act"], 1)

                def merged_high(m):
                    act.wait_ge(s["merged"], 4 * l + m + 1)
                    nc.scalar.activation(hH[:, 2 * m:2 * m + 2, :], hf[:, 2 * m:2 * m + 2, :], ACT.Copy,
                                         scale=0.5).then_inc(s["merged_high"], 1)

                for n in range(3, MIX_PIECES):
                    if 16 <= n <= 23:
                        h = n - 16
                        act.wait_ge(s["prob_t"], 8 * l + h + 1)
                        if h:
                            act.wait_ge(s["pv"], 8 * l + h)
                        nc.scalar.activation(probT[:], bank[6][:, 0:384], ACT.Copy).then_inc(s["prob_t_out"], 1)
                    if 14 <= n <= 21:
                        h = n - 14
                        act.wait_ge(s["max_done"], 2 * (8 * l + h) + 2)
                        for t, (a, z) in enumerate(((0, 128), (128, 384))):
                            nc.scalar.activation(prob[:, h % 2, a:z], bank[4 + h % 2][:, a:z], ACT.Exp,
                                                 bias=negmax[:, h % 2, t:t + 1],
                                                 accum_out=psum_[:, h % 2, t:t + 1]).then_inc(s["exp_done"], 1)
                    if n == 13:
                        act.wait_ge(s["pooled_ready"], l + 1)
                        nc.scalar.activation(pooled, fold(bank[3][:], 2), ACT.Copy).then_inc(s["pool_in_ready"], 1)
                    if n == 15:
                        act.wait_ge(s["y_full"], 2 * l + 1)
                        nc.scalar.activation(yH[:, 0:2, :], yf[:], ACT.Copy).then_inc(s["y_high_done"], 1)
                    if n >= 18 and n <= 24 and n % 2 == 0:
                        c = (n - 18) // 2
                        act.wait_ge(s["values_copied"], 4 * l + c + 1)
                        nc.scalar.activation(yH[:, 4 + c, :], attn[c % 2], ACT.Copy).then_inc(s["y_high_done"], 1)
                    if n == 20:
                        act.wait_ge(s["ln_zc"], 2 * l + 2)
                        nc.scalar.activation(cs[:], cv[:], ACT.Square).then_inc(s["ln_sq"], 1)
                    if n == 22:
                        act.wait_ge(s["ln_var"], l + 1)
                        nc.scalar.activation(rt[:, 0:S], bank[3][:, S:2 * S], ACT.Sqrt, bias=A(0, A_EPS),
                                             scale=1.0 / 256).then_inc(s["ln_root"], 1)
                    if n == 23:
                        act.wait_ge(s["ln_v"], 2 * l + 2)
                        nc.scalar.activation(cs[:], cv[:], ACT.Tanh, scale=0.5).then_inc(s["ln_th"], 1)
                    if n == 24:
                        act.wait_ge(s["y_full"], 2 * l + 2)
                        nc.scalar.activation(yH[:, 2:4, :], yf[:], ACT.Copy).then_inc(s["y_high_done"], 1)
                    if n == 27:
                        merged_high(2)
                        merged_high(3)
                    if 5 <= n <= 8:
                        u = n - 3
                        unit_ready(act, l, u)
                        nc.scalar.activation(qsq[:, u % 2, :], bank[UNIT_BANK[u]][:], ACT.Square).then_inc(s["qk_sq"], 1)
                    split_high(act, b + n)
                    if n == 4:
                        unit_ready(act, l, 1)
                        nc.scalar.activation(cs[:].rearrange("p c t -> p (c t)"), bank[1][:], ACT.Tanh,
                                             scale=0.5).then_inc(s["unit_used_act"], 1)
                    if 6 <= n <= 9:
                        u = n - 4
                        act.wait_ge(s["qk_stats"], 4 * l + u - 1)
                        if u > P_Q:
                            act.wait_ge(s["unit_used_dve"], len(DVE_UNITS) * l + DVE_UNITS.index(u - 1) + 1)
                        q = u < P_K
                        nc.scalar.activation(rt[:], bank[6 + u % 2][:], ACT.Sqrt,
                                             bias=A(0, A_EPS64 if q else A_EPS),
                                             scale=1.0 if q else 1.0 / HD).then_inc(s["qk_root"], 1)
                    if 9 <= n <= 11:
                        u = n - 3
                        unit_ready(act, l, u)
                        dst = pt_ if u == P_POOL else vt[:, :, 256 * (u - P_V):256 * (u - P_V) + 256]
                        nc.scalar.activation(dst, fold(bank[UNIT_BANK[u]][:], 2), ACT.Copy).then_inc(s["unit_used_act"], 1)
                    if 12 <= n <= 23:
                        gate_out(n - 3)
                    if n >= 17 and n <= 23 and n % 2 == 1:
                        c = (n - 17) // 2
                        act.wait_ge(s["pv"], 8 * l + 2 * c + 2)
                        if c >= 2:
                            act.wait_ge(s["y_low_done"], 6 * l + LOW_ORDER[4 + c - 2])
                        nc.scalar.activation(attn[c % 2], bank[7][:, 0:S], ACT.Copy).then_inc(s["values_copied"], 1)
                    if n == 26:
                        merged_high(0)
                        merged_high(1)
                squares(2 * l + 1, 0)
                squares(2 * l + 1, 1)
                if l == 0:
                    split_high(act, b + MIX_PIECES)
                squares(2 * l + 1, 2)
                if l == 0:
                    split_high(act, b + MIX_PIECES + 1)
                squares(2 * l + 1, 3)

            def dense():
                norm(1)

                def block_steps(par_, before):
                    act.wait_ge(s["used"], before * 3 + (DENSE0 + 2))
                    nc.scalar.activation(sl[:], bank[par_][:], ACT.Silu).then_inc(s["d_silu"], 1)
                    act.wait_ge(s["d_mult"], before + 1)
                    nc.scalar.activation(gH[:], gu[:], ACT.Copy).then_inc(s["d_high"], 1)

                with act.Fori(0, (DENSE_BLOCKS - 1) // 2) as i:
                    for u in range(2):
                        c = DENSE0 + 2 + 3 * u
                        split_high(act, c, i)
                        split_high(act, c + 1, i)
                        block_steps(u, i * 2 + u)
                        split_high(act, c + 2, i)
                split_high(act, DENSE0 + DENSE_PIECES - 1)
                block_steps(0, DENSE_BLOCKS - 1)
                split_high(act, BASE[1])
                split_high(act, BASE[1] + 1)
                for m in range(4):
                    squares(2, m)

            def experts():
                norm(3)
                split_high(act, MOE0)
                split_high(act, MOE0 + 1)
                for f in range(8):
                    act.wait_ge(s["fill"], f + 1)
                    dst = (htH if f < 4 else htL)[:, f % 4 // 2, 512 * (f % 2):512 * (f % 2) + 512]
                    nc.scalar.activation(dst, bank[f % 7][:], ACT.Copy).then_inc(s["fill_act"], 1)
                for f in range(8, 12):
                    act.wait_ge(s["fill"], f + 1)
                    dst = xacc[:, f % 4 // 2, 512 * (f % 2):512 * (f % 2) + 512]
                    nc.scalar.activation(dst, bank[f % 7][:], ACT.Copy).then_inc(s["fill_act"], 1)
                split_high(act, MOE0 + 2)
                act.wait_ge(s["r_lg"], 1)
                nc.scalar.activation(wt[:, 1, :], wt[:, 0, :], ACT.Exp).then_inc(s["r_exp"], 1)

                def gather_out(g, count):
                    act.wait_ge(s["m_gather"], count + g + 1)
                    dst = (hgH if g < 2 else hgL)[:, 4 * (g % 2):4 * (g % 2) + 4, :]
                    nc.scalar.activation(dst, fold(bank[GATHER_BANKS[g]][:], 4), ACT.Copy).then_inc(s["m_gout"], 1)

                def y_out(j):
                    act.wait_ge(s["m_zero"], 1)
                    act.wait_ge(s["used"], j * JOB_PIECES + MOE0)
                    for h in range(2):
                        nc.scalar.activation(ysb[:, 512 * h:512 * h + 512], bank[2 + h][:], ACT.Copy).then_inc(s["m_yout"], 1)

                def t_high(count):
                    act.wait_ge(s["m_t"], count)
                    nc.scalar.activation(gH[:], bank[4][:], ACT.Copy).then_inc(s["m_high"], 1)

                def silu(up_done):
                    act.wait_ge(s["used"], up_done)
                    nc.scalar.activation(sl[:], bank[0][:], ACT.Silu).then_inc(s["m_silu"], 1)

                for g in range(4):
                    gather_out(g, 0)

                def job(j):
                    r0, c = j * EXP_BLOCKS, MOE0
                    if not isinstance(j, int):
                        for k in range(SPLIT):
                            split_high(act, c + k, r0)
                    y_out(j)
                    split_high(act, c + 3, r0)
                    silu(j * JOB_PIECES + (MOE0 + 2))
                    split_high(act, c + 4, r0)
                    split_high(act, c + 5, r0)
                    with act.Fori(0, EXP_BLOCKS - 1) as i:
                        r = j * EXP_BLOCKS + i
                        split_high(act, c + 6, r)
                        split_high(act, c + 7, r)
                        split_high(act, c + 8, r)
                        t_high(r + 1)
                        silu(r * RAW + (MOE0 + 6))
                        split_high(act, c + 9, r)
                        split_high(act, c + 10, r)
                        split_high(act, c + 11, r)
                    t_high(j * EXP_BLOCKS + EXP_BLOCKS)
                    for g in range(4):
                        gather_out(g, j * 4 + 4)
                    act.wait_ge(s["m_permt"], j + 1)
                    nc.scalar.activation(permT[:], bank[1][:, 0:S], ACT.Copy).then_inc(s["m_ptout"], 1)

                job(0)
                act.wait_ge(s["jobs_ready"], 1)
                njobs = act.value_load(jobi[0:1, 12:13], min_val=EXPERTS, max_val=EXPERTS + EXTRA_JOBS)
                with act.Fori(1, njobs) as j:
                    job(j)
                y_out(njobs)

            act.wait_ge(s["ones_set"], 1)
            for m in range(4):
                squares(0, m)
            act.wait_ge(s["par_in"], 16)
            for l in range(DEPTH):
                nc.scalar.activation(half[:], A(l, A_BGATE, 24), ACT.Copy, scale=0.5).then_inc(s["wf_high"], 1)
                nc.scalar.activation(wfH[:], A(l, A_WF, SMALL), ACT.Copy).then_inc(s["wf_high"], 1)
                mixer(l)
                dense() if l == 0 else experts()

        @block.vector
        def _(dve):
            steps = [0]

            def step(ins):
                ins.then_inc(s["dve_step"], 1)
                steps[0] += 1

            def stepped():
                dve.wait_ge(s["dve_step"], steps[0])

            def norm(nn):
                dve.wait_ge(s["norm_root"], nn + 1)
                nc.vector.reciprocal(rinv[:, 0:S], rt[:, 0:S]).then_inc(s["norm_step"], 1)
                dve.wait_ge(s["norm_step"], nn + 1)

                def low(g):
                    dve.wait_ge(s["h_high_done"], 4 * nn + g + 1)
                    nc.vector.tensor_tensor(hL[:, 2 * g:2 * g + 2, :], hf[:, 2 * g:2 * g + 2, :],
                                            hH[:, 2 * g:2 * g + 2, :].bitcast(F32),
                                            ALU.subtract).then_inc(s["h_low_done"], 1)

                for k in range(KC):
                    nc.vector.scalar_tensor_tensor(
                        out=hf[:, k, :], in0=xT[:, k, :], scalar=A(nn // 2, (A_GMIX, A_GFFN)[nn % 2] + k),
                        in1=rinv[:, 0:S], op0=ALU.mult, op1=ALU.mult).then_inc(s["norm_h"], 1)
                    if k >= 3 and k % 2:
                        low(k // 2 - 1)
                low(3)

            def mixer(l):
                b = BASE[l]
                norm(2 * l)
                if l == 0:
                    split_low(dve, 0)
                    dve.wait_ge(s["f_raw"], l + 1)
                    nc.vector.tensor_copy(f8, bank[3][0:8, S:2 * S]).then_inc(s["f_copied"], 1)
                    split_low(dve, 1)
                split_low(dve, b + 2)
                step(nc.vector.memset(zp[:, :, 0:PAD], 0.0))
                if l:
                    dve.wait_ge(s["f_raw"], l + 1)
                    nc.vector.tensor_copy(f8, bank[3][0:8, S:2 * S]).then_inc(s["f_copied"], 1)
                dve.wait_ge(s["f_logits"], l + 1)
                step(nc.vector.tensor_tensor(
                    fg[:, 0, :].rearrange("p (t h) -> p t h", t=TT), bank[3][:, 256:272].rearrange("p (t h) -> p t h", t=TT),
                    A(l, A_BF, 8).unsqueeze(1).to_broadcast([P, TT, HEADS]), ALU.add))
                stepped()
                nc.vector.scalar_tensor_tensor(out=fg[:, 1, :], in0=fg[:, 0, :], scalar=-1.0, in1=fg[:, 0, :],
                                               op0=ALU.mult, op1=ALU.max).then_inc(s["f_soft"], 1)
                nc.vector.tensor_scalar(fg[:, 4, :], fg[:, 0, :], 0.0, None, ALU.min).then_inc(s["f_soft"], 1)

                taps = [(c, k) for k in range(TAPS) for c in range(CONVC)]
                tapped = [0]

                def run_taps(n):
                    for c, k in taps[tapped[0]:tapped[0] + n]:
                        tapped[0] += 1
                        w = A(l, A_CONVW + c * TAPS + k)
                        if k == 0:
                            step(nc.vector.tensor_scalar(cv[:, c, :], zp[:, c, 0:S], w, A(l, A_CONVB + c), ALU.mult, ALU.add))
                            continue
                        dve.wait_ge(s["dve_step"], steps[0] - (k < TAPS - 1))
                        ins = nc.vector.scalar_tensor_tensor(out=cv[:, c, :], in0=zp[:, c, k:k + S], scalar=w,
                                                             in1=cv[:, c, :], op0=ALU.mult, op1=ALU.add)
                        if k < TAPS - 1:
                            step(ins)
                        else:
                            ins.then_inc(s["ln_taps"], 1)

                def head_max(h):
                    dve.wait_ge(s["scores"], 8 * l + h + 1)
                    for t, (a, z) in enumerate(((0, 128), (128, 384))):
                        nc.vector.tensor_reduce(negmax[:, h % 2, t:t + 1], bank[4 + h % 2][:, a:z], AX_X, ALU.max,
                                                negate=True).then_inc(s["max_done"], 1)

                def head_norm(h):
                    dve.wait_ge(s["exp_done"], 2 * (8 * l + h) + 2)
                    step(nc.vector.reciprocal(pinv[:, h % 2, :], psum_[:, h % 2, :]))
                    stepped()
                    for t, (a, z) in enumerate(((0, 128), (128, 384))):
                        nc.vector.tensor_scalar(prob[:, h % 2, a:z], prob[:, h % 2, a:z], pinv[:, h % 2, t:t + 1],
                                                None, ALU.mult).then_inc(s["prob_done"], 1)

                def branch(u):
                    br, m = divmod(u - 21, 4)
                    unit_ready(dve, l, u)
                    dst = hf[:, 2 * m:2 * m + 2, :]
                    g = gate[:, 8 * br + 2 * m:8 * br + 2 * m + 2, :]
                    to = dst if br == 0 else g
                    ins = nc.vector.scalar_tensor_tensor(out=to, in0=g, scalar=1.0, in1=fold(bank[UNIT_BANK[u]][:], 2),
                                                         op0=ALU.add, op1=ALU.mult)
                    ins.then_inc(s["unit_used_dve"], 1)
                    if br:
                        dve.wait_ge(s["unit_used_dve"], len(DVE_UNITS) * l + DVE_UNITS.index(u) + 1)
                        ins = nc.vector.tensor_tensor(dst, dst, g, ALU.add)
                        if br == 2:
                            ins.then_inc(s["merged"], 1)
                        else:
                            step(ins)

                def residual(u):
                    m = u - 33
                    unit_ready(dve, l, u)
                    nc.vector.tensor_tensor(xT[:, 2 * m:2 * m + 2, :], xT[:, 2 * m:2 * m + 2, :],
                                            fold(bank[UNIT_BANK[u]][:], 2), ALU.add).then_inc(s["unit_used_dve"], 1)

                def merged_low(m):
                    dve.wait_ge(s["merged_high"], 4 * l + m + 1)
                    nc.vector.scalar_tensor_tensor(
                        out=hL[:, 2 * m:2 * m + 2, :], in0=hf[:, 2 * m:2 * m + 2, :], scalar=0.5,
                        in1=hH[:, 2 * m:2 * m + 2, :].bitcast(F32), op0=ALU.mult,
                        op1=ALU.subtract).then_inc(s["merged_low"], 1)

                for n in range(3, MIX_PIECES):
                    if 15 <= n <= 22:
                        head_norm(n - 15)
                    if 14 <= n <= 21:
                        head_max(n - 14)
                    if n == 14:
                        dve.wait_ge(s["pool_lin"], l + 1)
                        for c in range(2):
                            ins = nc.vector.tensor_scalar(yf[:, c, :], bank[3][:, c * S:c * S + S], A(l, A_PSCALE + c),
                                                          None, ALU.mult)
                        ins.then_inc(s["y_full"], 1)
                    if n == 16:
                        dve.wait_ge(s["y_high_done"], 6 * l + 1)
                        nc.vector.tensor_tensor(yL[:, 0:2, :], yf[:], yH[:, 0:2, :].bitcast(F32),
                                                ALU.subtract).then_inc(s["y_low_done"], 1)
                    if n >= 19 and n <= 25 and n % 2 == 1:
                        c = (n - 19) // 2
                        dve.wait_ge(s["y_high_done"], 6 * l + HIGH_ORDER[4 + c])
                        nc.vector.tensor_tensor(yL[:, 4 + c, :], attn[c % 2], yH[:, 4 + c, :].bitcast(F32),
                                                ALU.subtract).then_inc(s["y_low_done"], 1)
                    if n == 19:
                        dve.wait_ge(s["ln_mean"], l + 1)
                        for c in range(CONVC):
                            nc.vector.scalar_tensor_tensor(out=cv[:, c, :], in0=bank[3][:, 0:S], scalar=-1.0 / 256,
                                                           in1=cv[:, c, :], op0=ALU.mult, op1=ALU.add).then_inc(s["ln_zc"], 1)
                    if n == 22:
                        dve.wait_ge(s["ln_root"], l + 1)
                        step(nc.vector.reciprocal(rinv[:, 0:S], rt[:, 0:S]))
                        stepped()
                        for c in range(CONVC):
                            step(nc.vector.scalar_tensor_tensor(out=cv[:, c, :], in0=cv[:, c, :], scalar=A(l, A_LNG + c),
                                                                in1=rinv[:, 0:S], op0=ALU.mult, op1=ALU.mult))
                        stepped()
                        for c in range(CONVC):
                            nc.vector.tensor_scalar(cv[:, c, :], cv[:, c, :], A(l, A_LNB + c), None,
                                                    ALU.add).then_inc(s["ln_v"], 1)
                    if n == 23:
                        dve.wait_ge(s["ln_th"], l + 1)
                        step(nc.vector.scalar_tensor_tensor(out=cs[:], in0=cs[:], scalar=1.0, in1=cv[:],
                                                            op0=ALU.add, op1=ALU.mult))
                        stepped()
                        nc.vector.tensor_scalar(yf[:], cs[:], 0.5, None, ALU.mult).then_inc(s["y_full"], 1)
                    if n == 24:
                        dve.wait_ge(s["y_high_done"], 6 * l + HIGH_ORDER[2])
                        nc.vector.tensor_tensor(yL[:, 2:4, :], yf[:], yH[:, 2:4, :].bitcast(F32),
                                                ALU.subtract).then_inc(s["y_low_done"], 1)
                        for u in range(21, 25):
                            branch(u)
                        stepped()
                    if n == 25:
                        for u in range(25, 29):
                            branch(u)
                        stepped()
                    if n == 26:
                        branch(29)
                        branch(30)
                    if n == 27:
                        branch(31)
                        branch(32)
                        merged_low(2)
                        merged_low(3)
                    split_low(dve, b + n)
                    if n == 4:
                        dve.wait_ge(s["unit_used_act"], len(ACT_UNITS) * l + 1)
                        step(nc.vector.tensor_scalar(cs[:], cs[:], 0.5, 0.5, ALU.mult, ALU.add))
                        stepped()
                        nc.vector.tensor_tensor(zp[:, :, PAD:], cs[:], fold(bank[0][:], 2),
                                                ALU.mult).then_inc(s["unit_used_dve"], 1)
                        dve.wait_ge(s["unit_used_dve"], len(DVE_UNITS) * l + 1)
                    if 6 <= n <= 9:
                        u = n - 4
                        dve.wait_ge(s["qk_root"], 4 * l + u - 1)
                        step(nc.vector.reciprocal(rinv[:], rt[:]))
                        stepped()
                        nc.vector.scalar_tensor_tensor(
                            out=qk[:, 2 * (u - 2):2 * (u - 2) + 2, :], in0=fold(bank[UNIT_BANK[u]][:], 2),
                            scalar=A(l, A_QG if u < P_K else A_KG), in1=fold(rinv[:], 2),
                            op0=ALU.mult, op1=ALU.mult).then_inc(s["unit_used_dve"], 1)
                    if n == 7:
                        dve.wait_ge(s["act_step"], 2 * l + 2)
                        nc.vector.tensor_tensor(fg[:, 5, :], fg[:, 4, :], fg[:, 3, :],
                                                ALU.subtract).then_inc(s["decay_in"], 1)
                    if n == 26:
                        merged_low(0)
                        merged_low(1)
                    run_taps(TAPS_AT.get(n, 0))
                residual(33)
                residual(34)
                if l == 0:
                    split_low(dve, b + MIX_PIECES)
                residual(35)
                if l == 0:
                    split_low(dve, b + MIX_PIECES + 1)
                residual(36)
                dve.wait_ge(s["unit_used_dve"], len(DVE_UNITS) * (l + 1))

            def dense():
                norm(1)
                nc.vector.memset(zero[:].bitcast(F32), 0.0).then_inc(s["zeros"], 1)

                def block_steps(par_, before):
                    dve.wait_ge(s["d_silu"], before + 1)
                    nc.vector.tensor_tensor(gu[:], sl[:], bank[2 + par_][:], ALU.mult).then_inc(s["d_mult"], 1)
                    dve.wait_ge(s["d_high"], before + 1)
                    nc.vector.tensor_tensor(gL[:], gu[:], gH[:].bitcast(F32), ALU.subtract).then_inc(s["d_low"], 1)

                with dve.Fori(0, (DENSE_BLOCKS - 1) // 2) as i:
                    for u in range(2):
                        c = DENSE0 + 2 + 3 * u
                        split_low(dve, c, i)
                        split_low(dve, c + 1, i)
                        block_steps(u, i * 2 + u)
                        split_low(dve, c + 2, i)
                split_low(dve, DENSE0 + DENSE_PIECES - 1)
                block_steps(0, DENSE_BLOCKS - 1)
                split_low(dve, BASE[1])
                split_low(dve, BASE[1] + 1)
                for m in range(4):
                    if m < 3:
                        dve.wait_ge(s["d_y"], m + 1)
                    else:
                        dve.wait_ge(s["used"], BASE[1])
                    nc.vector.tensor_tensor(xT[:, 2 * m:2 * m + 2, :], xT[:, 2 * m:2 * m + 2, :], fold(bank[4 + m][:], 2),
                                            ALU.add).then_inc(s["d_res"], 1)
                dve.wait_ge(s["d_res"], 4)

            def route():
                iota8 = C(C_IOTA)[:, 0:8]
                step(nc.vector.memset(jobs[:], 0.0))
                step(nc.vector.memset(jobf[:], 0.0))
                dve.wait_ge(s["f_raw"], 3)
                nc.vector.tensor_copy(f8, bank[7][0:8, S:2 * S]).then_inc(s["f_copied"], 1)
                split_low(dve, MOE0)
                dve.wait_ge(s["r_logits"], 1)
                step(nc.vector.tensor_copy(lg[:], bank[7][:, 0:16].rearrange("p (t e) -> p t e", t=TT)))
                stepped()
                for t in range(TT):
                    step(nc.vector.max(top[:, t, :], lg[:, t, :]))
                stepped()
                for t in range(TT):
                    step(nc.vector.max_index(topi[:, t, :], top[:, t, :], lg[:, t, :]))
                nc.vector.tensor_tensor(wt[:, 0, :], top[:, :, 1], top[:, :, 0], ALU.subtract).then_inc(s["r_lg"], 1)
                stepped()
                step(nc.vector.tensor_copy(topf[:], topi[:]))
                stepped()
                for t in range(TT):
                    for a in range(2):
                        step(nc.vector.tensor_scalar(pick[:, a, t, :], iota8, topf[:, t, a:a + 1], None, ALU.is_equal))
                stepped()
                sel = jobs[:, 0, :, 0:8]
                nc.vector.tensor_tensor(sel, pick[:, 0], pick[:, 1], ALU.add).then_inc(s["r_pick"], 1)
                split_low(dve, MOE0 + 1)
                dve.wait_ge(s["r_rank"], 1)
                nc.vector.tensor_copy(jobs[:, 1, :, 0:8], bank[7][:, 32:48].rearrange("p (t e) -> p t e", t=TT)).then_inc(s["tables"], 1)
                step(nc.vector.tensor_copy(cnt[:, 0, :], bank[7][:, 64:72]))
                dve.wait_ge(s["tables"], 1)
                make_perm(0, perm, 0)

            def job_table():
                iota8 = C(C_IOTA)[:, 0:8]
                dve.wait_ge(s["r_exp"], 1)
                step(nc.vector.tensor_scalar(wt[:, 2, :], wt[:, 1, :], 1.0, None, ALU.add))
                stepped()
                step(nc.vector.reciprocal(wt[:, 3, :], wt[:, 2, :]))
                stepped()
                step(nc.vector.tensor_tensor(wt[:, 2, :], wt[:, 1, :], wt[:, 3, :], ALU.mult))
                stepped()
                for t in range(TT):
                    step(nc.vector.tensor_scalar(tmp8[:, t, :], pick[:, 1, t, :], wt[:, 2, t:t + 1], None, ALU.mult))
                stepped()
                for t in range(TT):
                    step(nc.vector.scalar_tensor_tensor(out=jobs[:, 2, t, 0:8], in0=pick[:, 0, t, :], scalar=wt[:, 3, t:t + 1],
                                                        in1=tmp8[:, t, :], op0=ALU.mult, op1=ALU.add))
                stepped()
                step(nc.vector.tensor_scalar(cnt[:, 1, :], cnt[:, 0, :], P + 0.5, None, ALU.is_gt))
                step(nc.vector.tensor_scalar(cnt[:, 4, :], iota8, -1.0, 16.0, ALU.mult, ALU.add))
                stepped()
                step(nc.vector.tensor_tensor(cnt[:, 2, :], cnt[:, 1, :], cnt[:, 4, :], ALU.mult))
                stepped()
                step(nc.vector.max(cnt[:, 3, :], cnt[:, 2, :]))
                step(nc.vector.tensor_reduce(cnt[:, 5, 0:1], cnt[:, 1, :], AX_X, ALU.add))
                stepped()
                for k in range(EXTRA_JOBS):
                    step(nc.vector.scalar_tensor_tensor(out=over[:, k, :], in0=cnt[:, 2, :], scalar=cnt[:, 3, k:k + 1],
                                                        in1=cnt[:, 1, :], op0=ALU.is_equal, op1=ALU.mult))
                stepped()
                for k in range(EXTRA_JOBS):
                    for q in range(3):
                        step(nc.vector.tensor_tensor(tmp8[:], jobs[:, q, :, 0:8],
                                                     over[:, k, :].unsqueeze(1).to_broadcast([P, TT, 8]), ALU.mult))
                        stepped()
                        step(nc.vector.tensor_reduce(jobs[:, q, :, 8 + k:9 + k], tmp8[:], AX_X, ALU.add))
                        stepped()
                step(nc.vector.tensor_scalar(jobs[:, 1, :, 8:8 + EXTRA_JOBS], jobs[:, 1, :, 8:8 + EXTRA_JOBS], -float(P), None, ALU.add))
                step(nc.vector.tensor_copy(jobf[:, 0:8], iota8))
                step(nc.vector.tensor_scalar(jobf[:, 8:8 + EXTRA_JOBS], cnt[:, 3, 0:EXTRA_JOBS], -1.0, 16.0, ALU.mult, ALU.add))
                step(nc.vector.tensor_scalar(jobf[:, 12:13], cnt[:, 5, 0:1], float(EXPERTS), None, ALU.add))
                stepped()
                step(nc.vector.tensor_scalar(jobf[:, 8:8 + EXTRA_JOBS], jobf[:, 8:8 + EXTRA_JOBS], float(EXPERTS - 1), None, ALU.min))
                stepped()
                nc.vector.tensor_copy(jobi[:], jobf[:]).then_inc(s["jobs_ready"], 1)

            def make_perm(q, dst, j):
                for t in range(TT):
                    nc.vector.tensor_scalar(dst[:, t, :], C(C_IOTA), jobs[:, 1, t, bass.ds(j, 1)], jobs[:, q, t, bass.ds(j, 1)],
                                            ALU.is_equal, ALU.mult).then_inc(s["m_perm"], 1)

            def add_rows(count):
                for q, b in enumerate((4, 7, 5, 6)):
                    dve.wait_ge(s["m_comb"], count + q + 1)
                    dst = xacc[:, q // 2, 512 * (q % 2):512 * (q % 2) + 512]
                    nc.vector.tensor_tensor(dst, dst, bank[b][:], ALU.add).then_inc(s["m_add"], 1)

            def experts():
                norm(3)
                nc.vector.memset(zero[:].bitcast(F32), 0.0).then_inc(s["zeros"], 1)
                nc.vector.memset(permT[:], 0.0).then_inc(s["m_ptout"], 1)
                route()
                split_low(dve, MOE0 + 2)
                job_table()
                stepped()
                dve.wait_ge(s["fill_act"], 12)

                def mult(count, up_done):
                    dve.wait_ge(s["used"], up_done)
                    dve.wait_ge(s["m_silu"], count)
                    nc.vector.tensor_tensor(gu[:], sl[:], bank[1][:], ALU.mult).then_inc(s["m_mult"], 1)

                def t_low(count):
                    dve.wait_ge(s["m_high"], count)
                    nc.vector.tensor_tensor(gL[:], bank[4][:], gH[:].bitcast(F32), ALU.subtract).then_inc(s["m_low"], 1)

                def job(j):
                    r0, c = j * EXP_BLOCKS, MOE0
                    for k in range(SPLIT if isinstance(j, int) else 0, 4):
                        split_low(dve, c + k, r0)
                    mult(r0 + 1, j * JOB_PIECES + (MOE0 + 4))
                    split_low(dve, c + 4, r0)
                    split_low(dve, c + 5, r0)
                    add_rows(j * 4)
                    make_perm(0, perm, j + 1)
                    make_perm(2, permG, j)
                    with dve.Fori(0, EXP_BLOCKS - 1) as i:
                        r = j * EXP_BLOCKS + i
                        split_low(dve, c + 6, r)
                        split_low(dve, c + 7, r)
                        split_low(dve, c + 8, r)
                        t_low(r + 1)
                        split_low(dve, c + 9, r)
                        mult(r + 2, r * RAW + (MOE0 + 8))
                        split_low(dve, c + 10, r)
                        split_low(dve, c + 11, r)
                    t_low(j * EXP_BLOCKS + EXP_BLOCKS)

                job(0)
                dve.wait_ge(s["jobs_ready"], 1)
                njobs = dve.value_load(jobi[0:1, 12:13], min_val=EXPERTS, max_val=EXPERTS + EXTRA_JOBS)
                with dve.Fori(1, njobs) as j:
                    job(j)
                add_rows(njobs * 4)

            nc.vector.memset(warm[:], 1.0).then_inc(s["ones_set"], 1)
            nc.vector.memset(ones[:], 1.0).then_inc(s["ones_set"], 1)
            dve.wait_ge(s["par_in"], 16)
            for m in range(4):
                dve.wait_ge(x_in[m], 16)
            for l in range(DEPTH):
                dve.wait_ge(s["wf_high"], 2 * l + 2)
                nc.vector.tensor_tensor(wfL[:], A(l, A_WF, SMALL), wfH[:].bitcast(F32), ALU.subtract).then_inc(s["wf_low"], 1)
                mixer(l)
                dense() if l == 0 else experts()

        @block.tensor
        def _(pe):
            def norm_stats(nn, m):
                pe.wait_ge(s["squares"], 4 * nn + m + 1)
                for k in (2 * m, 2 * m + 1):
                    ins = pe.matmul(bank[3][:, 0:S], ones[:], hf[:, k, :], start=k == 0, stop=k == KC - 1)
                if m == 3:
                    ins.then_inc(s["norm_stats"], 1)

            def small_h(dst, at, nn):
                terms = []
                for k in range(KC):
                    if k % 2 == 0:
                        pe.wait_ge(s["h_low_done"], 4 * nn + k // 2 + 1)
                    terms = [(wfH[:, at + 8 * k:at + 8 * k + P], wfL[:, at + 8 * k:at + 8 * k + P], hH[:, k, :], hL[:, k, :])]
                    ins = products(pe, dst, terms, start=k == 0, stop=k == KC - 1)
                ins.then_inc(s["f_raw"], 1)

            def small_turn(b, at, count, name):
                pe.wait_ge(s["f_copied"], count)
                for t in range(TT):
                    ins = pe.transpose(bank[b][:, at + 8 * t:at + 8 * t + 8], f8[:, t * P:t * P + P], C(C_IDENT)[0:8, 0:8])
                ins.then_inc(s[name], 1)

            def bank_free(l, u):
                v = UNIT_BEFORE[u]
                if v is not None:
                    who, name = (ACT_UNITS, "unit_used_act") if v in ACT_UNITS else (DVE_UNITS, "unit_used_dve")
                    pe.wait_ge(s[name], len(who) * l + who.index(v) + 1)

            def channel_unit(l, u, H, L, act_h, act_l, columns, between=None, before=None):
                bank_free(l, u)
                K = H.shape[1]
                for m in range(2):
                    if m and between:
                        between()
                    c0 = columns + m * P
                    for k in range(K):
                        if before and m == 0:
                            before(k)
                        ins = products(pe, bank[UNIT_BANK[u]][:, m * S:m * S + S], [
                            (H[:, k, c0:c0 + P], L[:, k, c0:c0 + P], act_h[:, k, :], act_l[:, k, :])],
                            start=k == 0, stop=k == K - 1)
                ins.then_inc(s["used" if UNIT_LAST[u] else "unit_part"], 1)

            def mixer(l):
                b = BASE[l]
                pe.wait_ge(s["wf_low"], l + 1)
                small_h(bank[3][:, S:2 * S], 0, 2 * l)

                def q_k_stats(u):
                    if l == 0 and u == P_Q:
                        pe.wait_ge(s["const_in"], 16)
                    pe.wait_ge(s["qk_sq"], 4 * l + u - 1)
                    pe.matmul(bank[6 + u % 2][:], C(C_HALVES), qsq[:, u % 2, :], start=True, stop=True).then_inc(s["qk_stats"], 1)

                def pool_means():
                    pe.wait_ge(s["unit_used_act"], len(ACT_UNITS) * l + 4)
                    pe.wait_ge(s["f_soft"], 2 * l + 2)
                    for c in range(2):
                        for g in range(2):
                            w = C_POOL + 3 * (2 * c + g)
                            lo = 128 * c + 64 * g
                            pe.matmul(bank[3][64 * g:64 * g + 64, c * S:c * S + S], pt_[:, 0, lo:lo + 64], C(w, 2),
                                      start=True, stop=False)
                            ins = pe.matmul(bank[3][64 * g:64 * g + 64, c * S + P:c * S + S], pt_[:, 1, lo:lo + 64], C(w + 2),
                                            start=False, stop=True)
                    ins.then_inc(s["pooled_ready"], 1)

                def pool_map():
                    pe.wait_ge(s["pool_in_ready"], l + 1)
                    for c in range(2):
                        ins = pe.matmul(bank[3][:, c * S:c * S + S], A(l, A_POOLW + P * c, P), pooled[:, c, :], start=True, stop=True)
                    ins.then_inc(s["pool_lin"], 1)

                def ln_sum(src, at, name):
                    for c in range(CONVC):
                        ins = pe.matmul(bank[3][:, at:at + S], C(C_ONES), src[:, c, :], start=c == 0, stop=c == 1)
                    ins.then_inc(s[name], 1)

                def head_scores(h):
                    pe.wait_ge(s["decays"], 3 * (8 * l + h) + 3)
                    if h >= 2:
                        pe.wait_ge(s["exp_done"], 2 * (8 * l + h - 2) + 2)
                    B = bank[4 + h % 2]
                    rows = slice(64 * (h % 2), 64 * (h % 2) + 64)
                    q, k = qk[rows, h // 2, :], qk[rows, 4 + h // 2, :]
                    pe.matmul(B[:, 0:128], q[:, 0:P], k[:, 0:P], start=True, stop=False)
                    pe.matmul(B[:, 0:128], decay[:, h % 2, 0, :], C(C_AFTER), start=False, stop=False)
                    pe.matmul(B[:, 0:128], ident, C(C_MASK), start=False, stop=True)
                    pe.matmul(B[:, 128:384], q[:, P:S], k, start=True, stop=False)
                    pe.matmul(B[:, 128:256], decay[:, h % 2, 2, :], C(C_AFTER), start=False, stop=False)
                    pe.matmul(B[:, 128:384], decay[:, h % 2, 1, :], C(C_ONES, 2), start=False, stop=False)
                    pe.matmul(B[:, 256:384], ident, C(C_MASK), start=False, stop=True).then_inc(s["scores"], 1)

                def head_turn(h):
                    pe.wait_ge(s["prob_done"], 2 * (8 * l + h) + 2)
                    if h >= 1:
                        pe.wait_ge(s["prob_t_out"], 8 * l + h)
                    for t in range(3):
                        ins = pe.transpose(bank[6][:, t * P:t * P + P], prob[:, h % 2, t * P:t * P + P], ident)
                    ins.then_inc(s["prob_t"], 1)

                def head_values(h):
                    pe.wait_ge(s["prob_t_out"], 8 * l + h + 1)
                    if h >= 2 and h % 2 == 0:
                        pe.wait_ge(s["values_copied"], 4 * l + h // 2)
                    rows = slice(64 * (h % 2), 64 * (h % 2) + 64)
                    v = slice(HD * h, HD * h + HD)
                    pe.matmul(bank[7][rows, 0:S], vt[:, 0, v], probT[:, 0:S], start=True, stop=False)
                    pe.matmul(bank[7][rows, P:S], vt[:, 1, v], probT[:, S:S + P], start=False,
                              stop=True).then_inc(s["pv"], 1)

                for n in range(P_BRPOOL):
                    H, L = take_piece(pe, b + n)
                    if n in (P_V, P_V + 1, P_POOL):
                        bank_free(l, n)
                        for t in range(TT):
                            if t and n == P_V:
                                q_k_stats(n - 1)
                            ins = products(pe, bank[UNIT_BANK[n]][:, t * 256:t * 256 + 256], [
                                (hH[:, k, t * P:t * P + P], hL[:, k, t * P:t * P + P], H[:, k, :], L[:, k, :])
                                for k in range(KC)])
                        ins.then_inc(s["used"], 1)
                    else:
                        channel_unit(l, n, H, L, hH, hL, 0, (lambda: q_k_stats(n - 1)) if 3 <= n <= 5 else None)
                    if n == 0:
                        if l == 0:
                            pe.wait_ge(s["const_in"], 16)
                        small_turn(3, S, l + 1, "f_logits")
                    if n == 9:
                        pool_means()
                    if n == 10:
                        pool_map()
                    if n == 15:
                        pe.wait_ge(s["y_full"], 2 * l + 1)
                        pe.wait_ge(s["ln_taps"], 2 * l + 2)
                        ln_sum(cv, 0, "ln_mean")
                    if n == 18:
                        pe.wait_ge(s["ln_sq"], l + 1)
                        ln_sum(cs, S, "ln_var")
                    if 10 <= n <= 17:
                        head_scores(n - 10)
                    if 12 <= n <= 19:
                        head_turn(n - 12)
                    if 13 <= n <= 20:
                        head_values(n - 13)
                u = 21
                for n in range(P_BRPOOL, P_OUT):
                    first, K, units = {P_BRPOOL: (0, 2, 4), P_BRCONV: (2, 2, 4), P_BRATTN: (4, 4, 2), P_BRATTN + 1: (4, 4, 2)}[n]
                    need = {P_BRPOOL: LOW_ORDER[0], P_BRCONV: LOW_ORDER[2], P_BRATTN: 6, P_BRATTN + 1: 6}[n]
                    pe.wait_ge(s["y_low_done"], 6 * l + need)
                    H, L = take_piece(pe, b + n, 0, K)
                    for m in range(units):
                        channel_unit(l, u, H, L, yH[:, first:first + K, :], yL[:, first:first + K, :], 256 * m)
                        u += 1
                for n in range(P_OUT, MIX_PIECES):
                    def part_ready(k):
                        if k % 2 == 0:
                            pe.wait_ge(s["merged_low"], 4 * l + k // 2 + 1)

                    H, L = take_piece(pe, b + n)
                    channel_unit(l, u, H, L, hH, hL, 0, before=part_ready if n == P_OUT else None)
                    u += 1
                    if n > P_OUT:
                        norm_stats(2 * l + 1, n - P_OUT - 1)
                norm_stats(2 * l + 1, 3)

            def zero_bank(b):
                return pe.matmul(bank[b][:], zero[:, 0:P], zero[:], start=True, stop=False)

            def dense():
                def up(c, r, b, first=False):
                    H, L = take_piece(pe, c, r)
                    for m in range(2):
                        for k in range(KC):
                            if first and m == 0 and k % 2 == 0:
                                pe.wait_ge(s["h_low_done"], 4 + k // 2 + 1)
                            ins = products(pe, bank[b][:, m * S:m * S + S], [
                                (H[:, k, m * P:m * P + P], L[:, k, m * P:m * P + P], hH[:, k, :], hL[:, k, :])],
                                start=k == 0, stop=k == KC - 1)
                    ins.then_inc(s["used"], 1)

                def down(c, r, count, stop=False):
                    H, L = take_piece(pe, c, r, 2)
                    pe.wait_ge(s["d_low"], count)
                    for m in range(KC):
                        ins = products(pe, bank[4 + m // 2][:, (m % 2) * S:(m % 2) * S + S], [
                            (H[:, k, m * P:m * P + P], L[:, k, m * P:m * P + P],
                             gH[:, k * S:k * S + S], gL[:, k * S:k * S + S]) for k in range(2)],
                            start=False, stop=stop and m % 2 == 1)
                        if stop and m in (1, 3, 5):
                            ins.then_inc(s["d_y"], 1)
                    ins.then_inc(s["used"], 1)

                up(DENSE0, 0, 0, first=True)
                up(DENSE0 + 1, 0, 2)
                pe.wait_ge(s["zeros"], 1)
                for m in range(4):
                    zero_bank(4 + m)
                with pe.Fori(0, (DENSE_BLOCKS - 1) // 2) as i:
                    for u in range(2):
                        c = DENSE0 + 2 + 3 * u
                        up(c, i, 1 - u)
                        up(c + 1, i, 3 - u)
                        down(c + 2, i, i * 2 + (u + 1))
                down(DENSE0 + DENSE_PIECES - 1, 0, DENSE_BLOCKS, stop=True)
                for m in range(4):
                    norm_stats(2, m)

            def experts():
                small_h(bank[7][:, S:2 * S], 64, 3)
                for f in range(12):
                    src = (hH, hL, xT)[f // 4]
                    if f >= 7:
                        pe.wait_ge(s["fill_act"], f - 6)
                    if f == 4:
                        small_turn(7, 0, 3, "r_logits")
                    t, half_ = f % 4 // 2, f % 2
                    for k in range(4):
                        a = src[:, 4 * half_ + k, t * P:t * P + P]
                        ins = pe.transpose(bank[f % 7][:, k * P:k * P + P], a if f >= 8 else a.bitcast(F32), ident)
                    ins.then_inc(s["fill"], 1)
                pe.wait_ge(s["r_pick"], 1)
                sel = [jobs[:, 0, t, 0:8] for t in range(TT)]
                pe.matmul(bank[7][:, 32:40], C(C_BEFORE), sel[0], start=True, stop=True)
                pe.matmul(bank[7][:, 40:48], C(C_ONES), sel[0], start=True, stop=False)
                pe.matmul(bank[7][:, 40:48], C(C_BEFORE), sel[1], start=False, stop=True)
                pe.matmul(bank[7][:, 64:72], C(C_ONES), sel[0], start=True, stop=False)
                pe.matmul(bank[7][:, 64:72], C(C_ONES), sel[1], start=False, stop=True).then_inc(s["r_rank"], 1)

                def gather(g):
                    src = htH if g < 2 else htL
                    for k in range(4):
                        ch = 4 * (g % 2) + k
                        for t in range(TT):
                            ins = pe.matmul(bank[GATHER_BANKS[g]][:, k * P:k * P + P], src[:, t, ch * P:ch * P + P],
                                            perm[:, t, :], start=t == 0, stop=t == TT - 1)
                    ins.then_inc(s["m_gather"], 1)

                def up(c, r, b):
                    for half_ in range(2):
                        H, L = take_piece(pe, c + half_, r, 4)
                        ins = products(pe, bank[b][:], [
                            (hgH[:, 4 * half_ + k, :], hgL[:, 4 * half_ + k, :], H[:, k, :], L[:, k, :]) for k in range(4)],
                            start=half_ == 0, stop=half_ == 1)
                        ins.then_inc(s["used"], 1)

                def turn(count):
                    pe.wait_ge(s["m_mult"], count)
                    for k in range(4):
                        ins = pe.transpose(bank[4][:, k * P:k * P + P], gu[:, k * P:k * P + P], ident)
                    ins.then_inc(s["m_t"], 1)

                def down(c, r, count, stop=False):
                    pe.wait_ge(s["m_low"], count)
                    for half_ in range(2):
                        H, L = take_piece(pe, c + half_, r, 2)
                        for n in range(2):
                            ins = products(pe, bank[2 + n][:], [
                                (gH[:, (2 * half_ + k) * P:(2 * half_ + k) * P + P], gL[:, (2 * half_ + k) * P:(2 * half_ + k) * P + P],
                                 H[:, k, 512 * n:512 * n + 512], L[:, k, 512 * n:512 * n + 512]) for k in range(2)],
                                start=False, stop=stop and half_ == 1)
                        ins.then_inc(s["used"], 1)

                def combine(count):
                    for q, b in enumerate((4, 7, 5, 6)):
                        ins = pe.matmul(bank[b][:], permT[:, (q // 2) * P:(q // 2) * P + P],
                                        ysb[:, 512 * (q % 2):512 * (q % 2) + 512], start=True, stop=True)
                        ins.then_inc(s["m_comb"], 1)

                pe.wait_ge(s["fill_act"], 8)
                pe.wait_ge(s["m_perm"], 2)
                for g in range(4):
                    gather(g)
                pe.wait_ge(s["zeros"], 2)
                pe.wait_ge(s["fill_act"], 12)
                for n in range(2):
                    ins = pe.matmul(bank[2 + n][:], zero[:, 0:P], zero[:], start=True, stop=True)
                ins.then_inc(s["m_zero"], 1)

                def job(j):
                    r0, c = j * EXP_BLOCKS, MOE0
                    pe.wait_ge(s["m_gout"], j * 4 + 4)
                    up(c, r0, 0)
                    up(c + 2, r0, 1)
                    pe.wait_ge(s["m_yout"], j * 2 + 2)
                    pe.wait_ge(s["m_ptout"], j + 1)
                    combine(j * 4)
                    zero_bank(2)
                    zero_bank(3)
                    with pe.Fori(0, EXP_BLOCKS - 1) as i:
                        r = j * EXP_BLOCKS + i
                        pe.wait_ge(s["m_silu"], r + 1)
                        up(c + 4, r, 0)
                        pe.wait_ge(s["m_add"], j * 4 + 4)
                        turn(r + 1)
                        up(c + 6, r, 1)
                        down(c + 8, r, r + 1)
                    turn(j * EXP_BLOCKS + EXP_BLOCKS)
                    pe.wait_ge(s["m_perm"], j * 4 + 4)
                    pe.wait_ge(s["m_silu"], r0 + EXP_BLOCKS)
                    for g in range(4):
                        gather(g)
                    pe.wait_ge(s["m_perm"], j * 4 + 6)
                    for t in range(TT):
                        ins = pe.transpose(bank[1][:, t * P:t * P + P], permG[:, t, :], ident)
                    ins.then_inc(s["m_permt"], 1)
                    down(c + JOB_PIECES - 2, r0, j * EXP_BLOCKS + EXP_BLOCKS, stop=True)

                job(0)
                pe.wait_ge(s["jobs_ready"], 1)
                njobs = pe.value_load(jobi[0:1, 12:13], min_val=EXPERTS, max_val=EXPERTS + EXTRA_JOBS)
                with pe.Fori(1, njobs) as j:
                    job(j)
                pe.wait_ge(s["m_yout"], njobs * 2 + 2)
                pe.wait_ge(s["m_ptout"], njobs + 1)
                combine(njobs * 4)

            pe.wait_ge(s["ones_set"], 2)
            for m in range(4):
                norm_stats(0, m)
            for l in range(DEPTH):
                mixer(l)
                dense() if l == 0 else experts()


def constants():
    row, col = np.arange(P)[:, None], np.arange(P)[None, :]
    blocks = [row == col, row // HD == col // HD, row <= col, np.ones((P, P)), row > col, row < col,
              np.where(col > row, NEG, 0.0), np.broadcast_to(col, (P, P))]
    for w in WINDOWS:
        lag = col - row
        seen = np.minimum(col + 1, w)
        blocks.append(((lag >= 0) & (lag < w)) / seen - (lag == 0))
        blocks.append((lag + P < w) / float(w) + 0.0 * col)
        blocks.append(((lag >= 0) & (lag < w)) / float(w) - (lag == 0))
    return np.ascontiguousarray(np.stack([np.asarray(b, np.float32) for b in blocks], 1))


def channels(a):
    return np.asarray(a).reshape(-1, P).T


def layer_params(i, l):
    out = np.zeros((P, N_PARAM), np.float32)

    def put(at, a):
        out[:, at:at + a.shape[1]] = a

    put(A_GMIX, channels(i["g_mix"][l]))
    put(A_GFFN, channels(i["g_ffn"][l]))
    put(A_BGATE, channels(i["b_gate"][l]))
    put(A_PSCALE, channels(i["pool_scale"][l]))
    for c in range(CONVC):
        put(A_CONVW + c * TAPS, np.asarray(i["conv_w"][l])[:, c * P:c * P + P].T)
    put(A_CONVB, channels(i["conv_b"][l]))
    put(A_LNG, channels(i["conv_ln_g"][l]))
    put(A_LNB, channels(i["conv_ln_b"][l]))
    put(A_QG, np.concatenate([i["q_norm_g"][l]] * 2)[:, None])
    put(A_KG, np.concatenate([i["k_norm_g"][l]] * 2)[:, None])
    put(A_BF, np.broadcast_to(np.asarray(i["b_forget"][l])[None, :], (P, HEADS)))
    out[:, A_EPS] = EPS
    out[:, A_EPS64] = EPS * HD
    for g in range(4):
        lo, at = HD * (g % 2), A_POOLW + P * (g // 2) + HD * (g % 2)
        out[lo:lo + HD, at:at + HD] = i["pool_w"][l][g]
    put(A_WF, np.asarray(i["w_in"][l])[:, OFF_F:OFF_G].reshape(KC, P, HEADS).transpose(1, 0, 2).reshape(P, -1))
    if l % 2:
        put(A_ROUTER, np.asarray(i["router_w"][l // 2]).reshape(KC, P, EXPERTS).transpose(1, 0, 2).reshape(P, -1))
    return out


def kernel(**inputs):
    import concourse.bacc as bacc
    from concourse.bass_utils import run_bass_kernel_spmd

    i = {k: np.asarray(v) for k, v in inputs.items()}
    arrays = {
        "xt": np.ascontiguousarray(i["x"][0].T.reshape(KC, P, S).transpose(1, 0, 2)),
        "consts": constants(),
        "params": np.ascontiguousarray(np.stack([layer_params(i, l) for l in range(DEPTH)], 1)),
    }
    for name in ("w_in", "w_br_pool", "w_br_conv", "w_br_attn", "w_out", "ffn_w1", "ffn_w3", "ffn_w2",
                 "exp_w1", "exp_w3", "exp_w2"):
        arrays[name] = np.ascontiguousarray(i[name])
    nc = bacc.Bacc("TRN2", target_bir_lowering=False, num_devices=1)
    aps = [nc.dram_tensor(n, a.shape, mybir.dt.from_np(a.dtype), kind="ExternalInput").ap() for n, a in arrays.items()]
    out = nc.dram_tensor("out", (1, S, D), F32, kind="ExternalOutput").ap()
    trunk(nc, *aps, out)
    return run_bass_kernel_spmd(nc, [arrays], core_ids=[0]).results[0]["out"]
```
